# Optimizing a Trainium2 kernel written in Bass

```python
import math
import jax, jax.numpy as jnp
from jax import lax
import numpy as np

D_MODEL = 1024
BATCH = 1
SEQ = 1024
DEPTH = 2

N_MIXERS = 2
N_POOL_LAYERS = (DEPTH + 1) // 2
N_MLSTM_LAYERS = DEPTH // 2

POOL_WINDOWS = (2, 4, 8, 16)
N_POOL_GROUPS = len(POOL_WINDOWS)
POOL_GROUP_DIM = D_MODEL // N_POOL_GROUPS

N_HEADS = 4
DV = D_MODEL // N_HEADS
DQK = DV // 2
CHUNK = 64
QK_W = N_HEADS * DQK
V_W = N_HEADS * DV
MLSTM_IN_W = 2 * QK_W + 2 * V_W + 2 * N_HEADS

D_FF = int(math.ceil(8 * D_MODEL / 3 / 256) * 256)

EPS = 1e-6

kernel_name = "hybrid_pool_mlstm_swiglu_trunk"

def rms_norm(x, g):
    xf = x.astype(jnp.float32)
    y = xf * lax.rsqrt(jnp.mean(xf * xf, axis=-1, keepdims=True) + EPS)
    return y.astype(x.dtype) * g

def pool_mixer(x, w, scale):
    B, S, D = x.shape
    xg = x.reshape(B, S, N_POOL_GROUPS, POOL_GROUP_DIM).astype(jnp.float32)
    cs = jnp.cumsum(xg, axis=1)
    pos = jnp.arange(1, S + 1, dtype=jnp.float32)
    outs = []
    for g, win in enumerate(POOL_WINDOWS):
        c = cs[:, :, g]
        prev = jnp.pad(c[:, :S - win], ((0, 0), (win, 0), (0, 0)))
        cnt = jnp.minimum(pos, float(win))[None, :, None]
        outs.append((c - prev) / cnt)
    pooled = jnp.stack(outs, axis=2) - xg
    y = jnp.einsum('bsgc,gcd->bsgd', pooled.astype(x.dtype), w).reshape(B, S, D)
    return y * scale

def mlstm_chunkwise(q, k, v, i_pre, logf):
    B, H, S, _ = q.shape
    nc = S // CHUNK

    def to_chunks(a):
        a = a.reshape(a.shape[:2] + (nc, CHUNK) + a.shape[3:])
        return jnp.moveaxis(a, 2, 0)

    xs = (to_chunks(q), to_chunks(k), to_chunks(v), to_chunks(i_pre), to_chunks(logf))
    causal = jnp.tril(jnp.ones((CHUNK, CHUNK), dtype=bool))

    def step(carry, inp):
        C, n, m = carry
        qc, kc, vc, ic, fc = inp
        b = jnp.cumsum(fc, axis=-1)
        log_d = b[..., :, None] - b[..., None, :] + ic[..., None, :]
        log_d = jnp.where(causal, log_d, -jnp.inf)
        log_inter = b + m[..., None]
        m_t = jnp.maximum(log_inter, jnp.max(log_d, axis=-1))
        d = jnp.exp(log_d - m_t[..., None])
        inter = jnp.exp(log_inter - m_t)
        s = jnp.einsum('bhtk,bhsk->bhts', qc, kc) * d
        num = inter[..., None] * jnp.einsum('bhtk,bhkv->bhtv', qc, C) \
            + jnp.einsum('bhts,bhsv->bhtv', s, vc)
        den = inter * jnp.einsum('bhtk,bhk->bht', qc, n) + jnp.sum(s, axis=-1)
        h = num / jnp.maximum(jnp.abs(den), jnp.exp(-m_t))[..., None]
        m_new = m_t[..., -1]
        decay = jnp.exp(b[..., -1] + m - m_new)
        w = jnp.exp(b[..., -1:] - b + ic - m_new[..., None])
        kw = kc * w[..., None]
        C_new = decay[..., None, None] * C + jnp.einsum('bhsk,bhsv->bhkv', kw, vc)
        n_new = decay[..., None] * n + jnp.sum(kw, axis=2)
        return (C_new, n_new, m_new), h

    init = (jnp.zeros((B, H, DQK, DV), jnp.float32),
            jnp.zeros((B, H, DQK), jnp.float32),
            jnp.zeros((B, H), jnp.float32))
    _, hs = lax.scan(step, init, xs)
    return jnp.moveaxis(hs, 0, 2).reshape(B, H, S, DV)

def mlstm_mixer(x, w_in, gate_bias, head_norm, w_out):
    B, S, _ = x.shape
    proj = x @ w_in
    q, k, v, o, gates = jnp.split(proj, [QK_W, 2 * QK_W, 2 * QK_W + V_W, 2 * QK_W + 2 * V_W], axis=-1)
    gates = gates.astype(jnp.float32) + gate_bias.astype(jnp.float32)
    i_pre = jnp.transpose(gates[..., :N_HEADS], (0, 2, 1))
    logf = jax.nn.log_sigmoid(jnp.transpose(gates[..., N_HEADS:], (0, 2, 1)))

    def heads(a, d):
        return jnp.transpose(a.reshape(B, S, N_HEADS, d), (0, 2, 1, 3)).astype(jnp.float32)

    qh = heads(q, DQK) * (DQK ** -0.5)
    kh = heads(k, DQK)
    vh = heads(v, DV)
    h = mlstm_chunkwise(qh, kh, vh, i_pre, logf)
    h = jnp.transpose(h, (0, 2, 1, 3))
    h = h * lax.rsqrt(jnp.mean(h * h, axis=-1, keepdims=True) + EPS)
    h = h.reshape(B, S, V_W).astype(x.dtype) * head_norm
    h = h * jax.nn.sigmoid(o)
    return h @ w_out

def swiglu(x, w_in, w_out):
    gu = x @ w_in
    g, u = gu[..., :D_FF], gu[..., D_FF:]
    return (jax.nn.silu(g) * u) @ w_out

def setup_inputs(seed: int = 0) -> dict:
    key = jax.random.key(seed)
    ks = jax.random.split(key, 16)
    f32 = jnp.float32
    nrm = lambda k, shape, s: jax.random.normal(k, shape, f32) * s
    fgate_bias = jnp.linspace(3.0, 6.0, N_HEADS, dtype=f32)
    gate_bias = jnp.concatenate([
        nrm(ks[6], (N_MLSTM_LAYERS, N_HEADS), 0.1),
        fgate_bias[None, :] + nrm(ks[7], (N_MLSTM_LAYERS, N_HEADS), 0.1)], axis=-1)
    return {
        "x": nrm(ks[0], (BATCH, SEQ, D_MODEL), 1.0),
        "pool_norm": 1.0 + nrm(ks[1], (N_POOL_LAYERS, D_MODEL), 0.02),
        "pool_w": nrm(ks[2], (N_POOL_LAYERS, N_POOL_GROUPS, POOL_GROUP_DIM, POOL_GROUP_DIM), POOL_GROUP_DIM ** -0.5),
        "pool_scale": 0.5 + nrm(ks[3], (N_POOL_LAYERS, D_MODEL), 0.05),
        "mlstm_norm": 1.0 + nrm(ks[4], (N_MLSTM_LAYERS, D_MODEL), 0.02),
        "mlstm_w_in": nrm(ks[5], (N_MLSTM_LAYERS, D_MODEL, MLSTM_IN_W), D_MODEL ** -0.5),
        "mlstm_gate_bias": gate_bias,
        "mlstm_head_norm": 1.0 + nrm(ks[8], (N_MLSTM_LAYERS, V_W), 0.02),
        "mlstm_w_out": nrm(ks[9], (N_MLSTM_LAYERS, V_W, D_MODEL), V_W ** -0.5),
        "ffn_norm": 1.0 + nrm(ks[10], (DEPTH, D_MODEL), 0.02),
        "ffn_w_in": nrm(ks[11], (DEPTH, D_MODEL, 2 * D_FF), D_MODEL ** -0.5),
        "ffn_w_out": nrm(ks[12], (DEPTH, D_FF, D_MODEL), D_FF ** -0.5),
        "final_norm": 1.0 + nrm(ks[13], (D_MODEL,), 0.02),
    }

def reference(x, pool_norm, pool_w, pool_scale, mlstm_norm, mlstm_w_in, mlstm_gate_bias,
              mlstm_head_norm, mlstm_w_out, ffn_norm, ffn_w_in, ffn_w_out, final_norm):
    h = x
    for i in range(DEPTH):
        j = i // N_MIXERS
        if i % N_MIXERS == 0:
            h = h + pool_mixer(rms_norm(h, pool_norm[j]), pool_w[j], pool_scale[j])
        else:
            h = h + mlstm_mixer(rms_norm(h, mlstm_norm[j]), mlstm_w_in[j], mlstm_gate_bias[j],
                                mlstm_head_norm[j], mlstm_w_out[j])
        h = h + swiglu(rms_norm(h, ffn_norm[i]), ffn_w_in[i], ffn_w_out[i])
    return rms_norm(h, final_norm)


_drawn_inputs = setup_inputs


def setup_inputs(seed=0):
    import zlib

    import numpy as np

    out = dict(_drawn_inputs(seed))
    spreads = {}
    factors = {'pool_norm': 4.416, 'mlstm_norm': 3.206, 'mlstm_head_norm': 6.903, 'final_norm': 2.741}
    for name, (base, spread) in spreads.items():
        noise = np.random.default_rng([zlib.crc32(name.encode()), seed]).standard_normal(out[name].shape)
        drawn = base * np.exp(spread * noise) if base else spread * noise
        out[name] = __import__('jax').numpy.asarray(drawn.astype(out[name].dtype))
    for name, factor in factors.items():
        out[name] = (out[name] * factor).astype(out[name].dtype)
    return out
```

```python
import concourse.bass as bass
from concourse import mybir
from concourse.alu_op_type import AluOpType as ALU

F32 = mybir.dt.float32
F32R = mybir.dt.float32r
ACT = mybir.ActivationFunctionType

P = 128
D = 1024
NT = 1024
HALF = 512
KD = D // P
D_FF = 2816
NJ = D_FF // P
FFN_BLOCKS = [(0, 8), (8, 7), (15, 7)]
HEADS = 4
DQK = 128
DV = 256
QSCALE = DQK ** -0.5
CH = 128
NCH = NT // CH
EPS = 1e-6
TINY = 2.0e-38
NEG = -3.0e38
GROUPS = 4
LONGEST = 16

T_POOL = 0
T_FFN0 = 2
N_FFN = 2 * NJ + 3 * KD
T_GATE = T_FFN0 + N_FFN
T_QKV = T_GATE + 1
T_O = T_QKV + 16
T_OUT = T_O + 8
T_FFN1 = T_OUT + 8
T_END = T_FFN1 + N_FFN

G_POOL, G_SCALE, G_MLSTM, G_HEAD, G_FFN0, G_FFN1, G_FINAL = range(7)


def unit(n, half):
    return 2 * n + 12 + half


SEED = 4
GATE_STEPS = 12
N_CONSTS = 5 + 6 * GROUPS


def lagged(h, c, lag):
    return (h, c - lag, h * NCH + (c - lag)) if c >= lag else (h - 1, c - lag + NCH, h * NCH + (c - lag))


def chunk_ok(h, c, lag):
    return not isinstance(h, int) or 0 <= h * NCH + c - lag < HEADS * NCH


class Semaphores:
    pass


def made(i):
    return i + (SEED + 1)


def freed(i):
    return i + (SEED - 1)


def build(nc, x, pool_norm, pool_w, pool_scale, mlstm_norm, mlstm_w_in, mlstm_gate_bias, mlstm_head_norm,
          mlstm_w_out, ffn_norm, ffn_w_in, ffn_w_out, final_norm, out):
    h_spill = nc.dram_tensor("h_spill", [P, KD, NT], F32, kind="Internal").ap()
    rows_dram = nc.dram_tensor("rows_dram", [HEADS, 2, NT], F32, kind="Internal").ap()

    base = (nc.sbuf_base + 31) // 32 * 32
    arena_bytes = 212768
    nc.alloc_sbuf_tensor("arena", [P, arena_bytes // 4], F32)
    cursor = [base]

    def at(name, shape, dt, offset=None):
        size = 4
        for s in shape[1:]:
            size *= s
        if offset is None:
            offset = cursor[0]
            cursor[0] += (size + 31) // 32 * 32
            assert cursor[0] <= base + arena_bytes, (name, cursor[0] - base)
        return nc.alloc_sbuf_tensor_at(name, shape, dt, offset=offset)

    o_xhi = base
    xhi = at("xhi", [P, KD, NT], F32R)
    o_xlo = cursor[0]
    xlo = at("xlo", [P, KD, NT], F32R)
    o_b = cursor[0]
    cursor[0] += 3 * 32768
    wraw = at("wraw", [P, 2, KD, P], F32)
    whi = [at(f"whi{s}", [P, KD, P], F32R) for s in range(2)]
    wlo = [at(f"wlo{s}", [P, KD, P], F32R) for s in range(2)]
    ident = at("ident", [P, P], F32)
    ones = at("ones", [P, P], F32)
    causal = at("causal", [P, P], F32)
    gain = at("gain", [P, 7, KD], F32)
    bias_i = at("bias_i", [P, 1], F32)
    bias_f = at("bias_f", [P, 1], F32)
    minus_half = at("minus_half", [P, 1], F32)
    cols = at("cols", [P, 3, NCH, HEADS], F32)
    m_prev = at("m_prev", [P, NCH], F32)
    rstd_tok = at("rstd_tok", [P, KD], F32)
    o_tmp = cursor[0]
    R = at("R", [P, NT], F32)
    gate_buf = at("gate_buf", [P, 2, HALF], F32)
    act_buf = at("act_buf", [P, 2, HALF], F32)
    sq = at("sq", [P, 2, HALF], F32)
    acc = at("acc", [P, NT], F32)

    h0 = at("h0", [P, KD, NT], F32, o_b + 65536)
    x_hi_of = [xhi, at("x_hi1", [P, KD, NT], F32R, o_b + 32768)]
    x_lo_of = [xlo, at("x_lo1", [P, KD, NT], F32R, o_b + 65536)]
    a_hi = [at("a_hi0", [P, KD, NT], F32R, o_b), xhi]
    a_lo = [at("a_lo0", [P, KD, NT], F32R, o_b + 32768), xlo]
    h1 = at("h1", [P, KD, NT], F32, o_b)
    qkv = at("qkv", [P, 16, NT], F32, o_b)
    sig_o = at("sig_o", [P, KD, NT], F32, o_b + 65536)
    gi = at("gi", [P, NT], F32, o_b + 65536)
    lf = at("lf", [P, NT], F32, o_b + 65536 + 4096)
    bb = at("bb", [P, NT], F32, o_b + 65536 + 8192)
    mm = at("mm", [P, NT], F32, o_b + 65536 + 12288)
    ri = at("ri", [P, 2, NT], F32, o_b + 65536 + 16384)
    uu = at("uu", [P, NT], F32, o_b + 65536 + 24576)
    ww = at("ww", [P, NT], F32, o_b + 65536 + 28672)
    x_tok = at("x_tok", [P, KD, D], F32, o_b + 32768)
    pool_hi_buf = at("pool_hi_buf", [P, 4, NT], F32R, o_b)
    pool_lo_buf = at("pool_lo_buf", [P, 4, NT], F32R, o_b + 16384)
    gain_rows = at("gain_rows", [P, P], F32, o_tmp)
    inv_count = at("inv_count", [P, LONGEST], F32, o_tmp + 512)
    win_main = at("win_main", [P, GROUPS, P], F32, o_tmp + 4096)
    win_first = at("win_first", [P, GROUPS, P], F32, o_tmp + 6144)
    win_prev = at("win_prev", [P, GROUPS, LONGEST], F32, o_tmp + 8192)
    tok_stat = at("tok_stat", [P, 2, KD], F32, o_tmp + 8192 + 512)
    square_bin = at("square_bin", [P, D], F32, o_xlo)
    x_fin = at("x_fin", [P, KD, NT], F32, o_b + 32768)
    out_rows = at("out_rows", [P, 2, D], F32, o_b + 65536)
    cursor_core = [o_tmp]

    def core(name, shape):
        t = at(name, shape, F32, cursor_core[0])
        size = 4
        for s in shape[1:]:
            size *= s
        cursor_core[0] += (size + 31) // 32 * 32
        assert cursor_core[0] <= base + arena_bytes
        return t

    bc = core("bc", [P, 4, 2, CH])
    stage = core("stage", [P, 2, 4, CH])
    kwv = core("kwv", [P, 2, CH + DV + 1])
    dmat = core("dmat", [P, 2, CH])
    smat = core("smat", [P, 2, CH])
    qs = core("qs", [P, 2, CH])
    state = core("state", [P, DV + 1])
    hn = core("hn", [P, 2, DV])
    yt = core("yt", [P, 2, 2, CH])
    tiny = core("tiny", [P, 2, 8])
    core_bin = core("core_bin", [P, DV])

    bank = [nc.alloc_psum_tensor(f"bank{i}", [P, HALF], F32) for i in range(8)]

    s = Semaphores()
    x_loaded = [nc.alloc_semaphore(f"x_loaded{t}") for t in range(KD)]
    s.gains_loaded = nc.alloc_semaphore("gains_loaded")
    s.bias_loaded = nc.alloc_semaphore("bias_loaded")
    s.gate_i_loaded = nc.alloc_semaphore("gate_i_loaded")
    s.raw_even = nc.alloc_semaphore("raw_even")
    s.raw_odd = nc.alloc_semaphore("raw_odd")
    s.w_hi = nc.alloc_semaphore("w_hi")
    s.w_ready = nc.alloc_semaphore("w_ready")
    s.unit_done = nc.alloc_semaphore("unit_done")
    s.unit_read = nc.alloc_semaphore("unit_read")
    s.consts = nc.alloc_semaphore("consts")
    s.gains_t = nc.alloc_semaphore("gains_t")
    s.gains_ready = nc.alloc_semaphore("gains_ready")
    s.xt_done = nc.alloc_semaphore("xt_done")
    s.xt_read = nc.alloc_semaphore("xt_read")
    s.x_ssq = nc.alloc_semaphore("x_ssq")
    s.x_var = nc.alloc_semaphore("x_var")
    s.x_rstd = nc.alloc_semaphore("x_rstd")
    s.xs_ready = nc.alloc_semaphore("xs_ready")
    s.pool_done = nc.alloc_semaphore("pool_done")
    s.sq_done = nc.alloc_semaphore("sq_done")
    s.acc_done = nc.alloc_semaphore("acc_done")
    s.acc_zeroed = nc.alloc_semaphore("acc_zeroed")
    s.stat_done = nc.alloc_semaphore("stat_done")
    s.var_ready = nc.alloc_semaphore("var_ready")
    s.sd_ready = nc.alloc_semaphore("sd_ready")
    s.rstd_ready = nc.alloc_semaphore("rstd_ready")
    s.pool_hi = nc.alloc_semaphore("pool_hi")
    s.pool_ready = nc.alloc_semaphore("pool_ready")
    s.x_hi = nc.alloc_semaphore("x_hi")
    s.x_ready = nc.alloc_semaphore("x_ready")
    s.silu_done = nc.alloc_semaphore("silu_done")
    s.silu_scaled = nc.alloc_semaphore("silu_scaled")
    s.act_hi = nc.alloc_semaphore("act_hi")
    s.a_ready = nc.alloc_semaphore("a_ready")
    s.spilled = nc.alloc_semaphore("spilled")
    s.h_back = nc.alloc_semaphore("h_back")
    s.rows_out = nc.alloc_semaphore("rows_out")
    s.gate_chain = nc.alloc_semaphore("gate_chain")
    s.gate_act = nc.alloc_semaphore("gate_act")
    s.rows_final = nc.alloc_semaphore("rows_final")
    s.cols_done = nc.alloc_semaphore("cols_done")
    s.cols_ready = nc.alloc_semaphore("cols_ready")
    s.o_sig = nc.alloc_semaphore("o_sig")
    s.o_ready = nc.alloc_semaphore("o_ready")
    s.staged = nc.alloc_semaphore("staged")
    s.tr_done = nc.alloc_semaphore("tr_done")
    s.kw_ready = nc.alloc_semaphore("kw_ready")
    s.v_ready = nc.alloc_semaphore("v_ready")
    s.factor_chain = nc.alloc_semaphore("factor_chain")
    s.den_ready = nc.alloc_semaphore("den_ready")
    s.bc0 = nc.alloc_semaphore("bc0")
    s.bc1 = nc.alloc_semaphore("bc1")
    s.bc2 = nc.alloc_semaphore("bc2")
    s.bc3 = nc.alloc_semaphore("bc3")
    s.z_ready = nc.alloc_semaphore("z_ready")
    s.d_ready = nc.alloc_semaphore("d_ready")
    s.st_done = nc.alloc_semaphore("st_done")
    s.s_ready = nc.alloc_semaphore("s_ready")
    s.qs_ready = nc.alloc_semaphore("qs_ready")
    s.num_done = nc.alloc_semaphore("num_done")
    s.cupd_done = nc.alloc_semaphore("cupd_done")
    s.c_updated = nc.alloc_semaphore("c_updated")
    s.ssq_ready = nc.alloc_semaphore("ssq_ready")
    s.rs_ready = nc.alloc_semaphore("rs_ready")
    s.hn_ready = nc.alloc_semaphore("hn_ready")
    s.ht_done = nc.alloc_semaphore("ht_done")
    s.y_ready = nc.alloc_semaphore("y_ready")
    s.y_hi = nc.alloc_semaphore("y_hi")
    s.y_lo = nc.alloc_semaphore("y_lo")
    s.core_consts = nc.alloc_semaphore("core_consts")
    s.waits_passed = nc.alloc_semaphore("waits_passed")
    s.fin_scaled = nc.alloc_semaphore("fin_scaled")
    s.var_tok = nc.alloc_semaphore("var_tok")
    s.sd_tok = nc.alloc_semaphore("sd_tok")
    s.rstd_tok_ready = nc.alloc_semaphore("rstd_tok_ready")
    s.ft_done = nc.alloc_semaphore("ft_done")
    s.ft_read_v = nc.alloc_semaphore("ft_read_v")
    s.ft_read_a = nc.alloc_semaphore("ft_read_a")
    s.out_even = nc.alloc_semaphore("out_even")
    s.out_odd = nc.alloc_semaphore("out_odd")
    raw_loaded = [s.raw_even, s.raw_odd]
    out_stored = [s.out_even, s.out_odd]
    bc_loaded = [s.bc0, s.bc1, s.bc2, s.bc3]
    halves = [slice(0, HALF), slice(HALF, NT)]

    def blk3(ap):
        return ap.rearrange("p (a n) -> p a n", a=1)

    def one(t, c, cols_):
        return t[:, bass.ds(c, 1), cols_]

    w_in_view = [ffn_w_in[l].rearrange("(k p) m -> p k m", p=P) for l in range(2)]
    w_out_view = [ffn_w_out[l].rearrange("(k p) m -> p k m", p=P) for l in range(2)]
    w_mix = mlstm_w_in[0].rearrange("(k p) m -> p k m", p=P)
    w_mix_out = mlstm_w_out[0].rearrange("(k p) m -> p k m", p=P)

    ffn_stages = []
    for l, n in ((0, T_FFN0), (1, T_FFN1)):
        for b, (j0, nb) in enumerate(FFN_BLOCKS):
            ffn_stages.append((l, n, j0, nb, b == 0, b == len(FFN_BLOCKS) - 1))
            n += 2 * nb + KD

    h_of = [h0, h1]
    block = nc.Block()
    blk = block.__enter__()

    @blk.sync
    def _(sp):
        for t in range(KD):
            sp.dma_start(x_tok[:, t, :], x[0, t * P:(t + 1) * P, :]).then_inc(x_loaded[t], 16)
        for r, g in enumerate([pool_norm[0], pool_scale[0], mlstm_norm[0], mlstm_head_norm[0], ffn_norm[0],
                               ffn_norm[1], final_norm]):
            sp.dma_start(gain_rows[r * KD:(r + 1) * KD, :], g.rearrange("(k p) -> k p", p=P)) \
              .then_inc(s.gains_loaded, 16)
        with nc.allow_non_contiguous_dma(reason="eight biases, one per partition"):
            for bias, h in ((bias_i, 0), (bias_f, HEADS)):
                sp.dma_start(bias[0:HEADS, :], mlstm_gate_bias[0, h:h + HEADS].rearrange("(h a) -> h a", a=1)) \
                  .then_inc(s.bias_loaded, 16)
        for t in range(2):
            sp.dma_start(wraw[:, t, :, :].rearrange("p (a b) m -> p a (b m)", b=2),
                         pool_w[0, 2 * t:2 * t + 2].rearrange("g (k p) m -> p (g k) m", p=P)) \
              .then_inc(raw_loaded[t], 16)

        def load(n, par, src, nb=KD):
            sp.wait_ge(s.w_ready, n - 1)
            sp.dma_start(wraw[:, par, 0:nb, :], src).then_inc(raw_loaded[par], 16)

        def ffn_loads(stage):
            l, n0, j0, nb, _, _ = stage
            with sp.Fori(0, nb) as j:
                for part in range(2):
                    load(n0 + part + 2 * j, (n0 + part) % 2,
                         w_in_view[l][:, :, bass.ds(j * P + (part * D_FF + j0 * P), P)])
            with sp.Fori(0, KD // 2) as c:
                for part in range(2):
                    load(n0 + 2 * nb + part + 2 * c, (n0 + part) % 2,
                         w_out_view[l][:, j0:j0 + nb, bass.ds(c * (2 * P) + part * P, P)], nb)

        for st in ffn_stages[:3]:
            ffn_loads(st)
        sp.wait_ge(s.w_ready, T_GATE - 1)
        gate_cols = 2 * HEADS * DQK + 2 * HEADS * DV
        sp.dma_start(wraw[:, T_GATE % 2, :, 0:HEADS], w_mix[:, :, gate_cols:gate_cols + HEADS]) \
          .then_inc(s.gate_i_loaded, 16)
        sp.wait_ge(s.gate_i_loaded, 16)
        sp.dma_start(wraw[:, T_GATE % 2, :, 32:32 + HEADS], w_mix[:, :, gate_cols + HEADS:gate_cols + 2 * HEADS]) \
          .then_inc(raw_loaded[T_GATE % 2], 16)

        def mix_loads(n0, c0, count):
            with sp.Fori(0, count // 2) as c:
                for part in range(2):
                    load(n0 + part + 2 * c, (n0 + part) % 2,
                         w_mix[:, :, bass.ds(c * (2 * P) + (c0 + part) * P, P)])

        mix_loads(T_QKV, 0, 16)
        sp.wait_ge(s.rows_final, 3)
        sp.dma_start(rows_dram, ri[0:HEADS, :, :]).then_inc(s.rows_out, 16)
        mix_loads(T_O, 16, 8)
        load(T_OUT, T_OUT % 2, w_mix_out[:, :, 0:P])
        sp.wait_ge(s.rows_out, 16)
        sp.wait_ge(s.o_ready, 16)
        sp.wait_ge(s.core_consts, 2)
        with sp.Fori(0, HEADS) as h:
            for c in range(NCH):
                sp.wait_ge(s.c_updated, h * NCH + (c + 1))
                sp.dma_start(bc[:, c % 4, :, :],
                             rows_dram[bass.ds(h, 1), :, c * CH:(c + 1) * CH].to_broadcast([P, 2, CH])) \
                  .then_inc(bc_loaded[c % 4], 16)
        sp.wait_ge(s.staged, 2 * SEED + 2 * HEADS * NCH)
        sp.wait_ge(s.spilled, 16 * KD)
        sp.dma_start(h1[:, :, :], h_spill).then_inc(s.h_back, 16)
        load(T_OUT + 1, (T_OUT + 1) % 2, w_mix_out[:, :, P:2 * P])
        with sp.Fori(1, KD // 2) as c:
            for part in range(2):
                load(T_OUT + part + 2 * c, (T_OUT + part) % 2,
                     w_mix_out[:, :, bass.ds(c * (2 * P) + part * P, P)])
        for st in ffn_stages[3:]:
            ffn_loads(st)
        for t in range(KD):
            sp.wait_ge(s.ft_read_v, t + 1)
            sp.wait_ge(s.ft_read_a, t + 1)
            sp.dma_start(out[0, t * P:(t + 1) * P, :], out_rows[:, t % 2, :]).then_inc(out_stored[t % 2], 16)
        for par in range(2):
            sp.wait_ge(out_stored[par], 16 * KD // 2)

    @blk.gpsimd
    def _(pool):
        g = nc.gpsimd
        for sem in (s.tr_done, s.z_ready, s.d_ready, s.st_done, s.s_ready, s.qs_ready, s.num_done, s.kw_ready,
                    s.v_ready, s.cupd_done, s.c_updated, s.hn_ready, s.ht_done, s.y_ready, s.y_hi, s.y_lo, s.ssq_ready,
                    s.den_ready, s.rs_ready):
            pool.sem_inc(sem, SEED)
        pool.sem_inc(s.staged, 2 * SEED)
        g.memset(ident[:, :], 0.0).then_inc(s.consts, 1)
        g.memset(ones[:, :], 1.0).then_inc(s.consts, 1)
        g.memset(causal[:, :], 0.0).then_inc(s.consts, 1)
        pool.wait_ge(s.consts, 3)
        g.affine_select(out=ident[:, :], in_=ident[:, :], compare_op=ALU.not_equal, fill=1.0, base=0,
                        pattern=[[-1, P]], channel_multiplier=1).then_inc(s.consts, 1)
        g.affine_select(out=causal[:, :], in_=causal[:, :], compare_op=ALU.is_ge, fill=NEG, base=0,
                        pattern=[[1, P]], channel_multiplier=-1).then_inc(s.consts, 1)
        g.memset(minus_half[:, :], -0.5)
        for t in range(LONGEST):
            g.memset(inv_count[:, t:t + 1], 1.0 / (t + 1))
        for gr in range(GROUPS):
            win = 2 << gr
            g.memset(win_main[:, gr, :], 1.0 / win)
            g.memset(win_first[:, gr, win:], 1.0 / win)
            g.memset(win_prev[:, gr, :], 1.0 / win).then_inc(s.consts, 1)
        pool.wait_ge(s.consts, 5 + GROUPS)
        for gr in range(GROUPS):
            win = 2 << gr
            g.tensor_copy(win_first[:, gr, 0:win], inv_count[:, 0:win]).then_inc(s.consts, 1)
        pool.wait_ge(s.consts, 5 + 2 * GROUPS)
        for gr in range(GROUPS):
            win = 2 << gr
            for m in (win_main, win_first):
                g.affine_select(out=m[:, gr, :], in_=m[:, gr, :], compare_op=ALU.is_ge, fill=0.0, base=0,
                                pattern=[[1, P]], channel_multiplier=-1)
            g.affine_select(out=win_prev[:, gr, :], in_=win_prev[:, gr, :], compare_op=ALU.is_ge, fill=0.0,
                            base=win - 1 - P, pattern=[[-1, LONGEST]], channel_multiplier=1).then_inc(s.consts, 1)
        pool.wait_ge(s.consts, 5 + 3 * GROUPS)
        for gr in range(GROUPS):
            win = 2 << gr
            for m in (win_main, win_first):
                last = g.affine_select(out=m[:, gr, :], in_=m[:, gr, :], compare_op=ALU.is_ge, fill=0.0,
                                       base=win - 1, pattern=[[-1, P]], channel_multiplier=1)
            last.then_inc(s.consts, 1)
        pool.wait_ge(s.consts, 5 + 4 * GROUPS)
        for gr in range(GROUPS):
            for m in (win_main, win_first):
                g.tensor_tensor(m[:, gr, :], m[:, gr, :], ident[:, :], ALU.subtract).then_inc(s.consts, 1)
        for t in range(KD):
            pool.wait_ge(s.x_var, t + 1)
            g.tensor_tensor(tok_stat[:, 1, t:t + 1], tok_stat[:, 0, t:t + 1], minus_half[:, :], ALU.pow) \
             .then_inc(s.x_rstd, 1)
        pool.wait_ge(s.o_ready, 16)
        for p in range(2):
            g.memset(kwv[:, p, CH + DV:CH + DV + 1], 1.0).then_inc(s.core_consts, 1)
        pool.wait_ge(s.core_consts, 2)

        def chunk_step(h, c):
            if chunk_ok(h, c, 0):
                i, tok = h * NCH + c, slice(c * CH, (c + 1) * CH)
                pool.wait_ge(s.st_done, freed(i))
                pool.wait_ge(s.qs_ready, freed(i))
                g.tensor_copy(stage[:, c % 2, 0:1, :], qkv[:, bass.ds(h, 1), tok])
                g.tensor_copy(stage[:, c % 2, 1:2, :], qkv[:, bass.ds(h + HEADS, 1), tok]).then_inc(s.staged, 1)
                g.tensor_copy(stage[:, c % 2, 2:4, :], qkv[:, bass.ds(h * 2 + 2 * HEADS, 2), tok]) \
                 .then_inc(s.staged, 1)
            if chunk_ok(h, c, 1):
                hh, cc, i = lagged(h, c, 1)
                ty = tiny[:, cc % 2, :]
                pool.wait_ge(s.den_ready, made(i))
                pool.wait_ge(s.ssq_ready, made(i))
                pool.wait_ge(s.hn_ready, freed(i))

                def link(step, ins):
                    ins.then_inc(s.factor_chain, 1)
                    pool.wait_ge(s.factor_chain, i * 5 + step)

                link(1, g.tensor_copy(ty[:, 7:8], cols[:, 2, cc, bass.ds(hh, 1)]))
                pool.sem_inc(s.waits_passed, 1)
                link(2, g.tensor_scalar(ty[:, 2:3], ty[:, 0:1], ty[:, 7:8], None, ALU.max))
                link(3, g.tensor_tensor(ty[:, 3:4], ty[:, 2:3], ty[:, 2:3], ALU.mult))
                pool.sem_inc(s.waits_passed, 1)
                link(4, g.tensor_scalar(ty[:, 4:5], ty[:, 3:4], EPS, TINY, ALU.mult, ALU.add))
                link(5, g.tensor_tensor(ty[:, 5:6], ty[:, 1:2], ty[:, 4:5], ALU.add))
                g.tensor_tensor(ty[:, 6:7], ty[:, 5:6], minus_half[:, :], ALU.pow).then_inc(s.rs_ready, 1)

        for c in range(NCH):
            chunk_step(0, c)
        with pool.Fori(1, HEADS) as h:
            for c in range(NCH):
                chunk_step(h, c)
        chunk_step(HEADS, 0)

    @blk.tensor
    def _(pe):
        mmul = nc.tensor.matmul
        pe.wait_ge(s.consts, 5)
        for t in range(KD):
            pe.wait_ge(x_loaded[t], 16)
            for part in range(2):
                k = 2 * t + part
                if k >= 4:
                    pe.wait_ge(s.xt_read, k - 3)
                for b in range(4):
                    last = nc.tensor.transpose(bank[k % 4][:, b * P:(b + 1) * P],
                                               x_tok[:, t, (4 * part + b) * P:(4 * part + b + 1) * P], ident[:, :])
                last.then_inc(s.xt_done, 1)
        pe.wait_ge(s.gains_loaded, 16 * 7)
        nc.tensor.transpose(bank[7][:, 0:56], gain_rows[0:56, :], ident[0:56, 0:56]).then_inc(s.gains_t, 1)

        def stats(index):
            for half in range(2):
                pe.wait_ge(s.acc_done, 2 * KD * (index + 1) - 1 + half)
                mmul(bank[4 + half][:, :], ones[:, :], acc[:, halves[half]], start=True, stop=True) \
                    .then_inc(s.stat_done, 1)

        def pool_block(c):
            g = c // 2
            for half in range(2):
                k = 2 * c + half
                b = bank[4 + k % 4]
                if k >= 4:
                    pe.wait_ge(s.pool_ready, k - 3)
                for t in range(4):
                    tt = 4 * half + t
                    if c == 0:
                        pe.wait_ge(s.xs_ready, tt + 1)
                    mmul(b[:, t * P:(t + 1) * P], x_tok[:, tt, c * P:(c + 1) * P],
                         (win_main if tt else win_first)[:, g, :], start=t == 0, stop=False)
                    if tt:
                        last = mmul(b[:, t * P:t * P + LONGEST], x_tok[:, tt - 1, c * P:(c + 1) * P],
                                    win_prev[:, g, :], start=False, stop=t == 3)
                last.then_inc(s.pool_done, 1)

        def pool_products(g):
            tile, row = g // 2, 2 * (g % 2)
            pe.wait_ge(s.w_ready, tile + 1)
            for m in range(2):
                for half in range(2):
                    u = 4 * g + 2 * m + half
                    if u >= 4:
                        pe.wait_ge(s.unit_read, u - 3)
                    else:
                        pe.wait_ge(s.xt_read, 2 * KD)
                    for k in range(2):
                        pe.wait_ge(s.pool_ready, 2 * (2 * g + k) + half + 1)
                        wh, wl = (w[tile][:, :, :].rearrange("p (a b) m -> p a (b m)", b=2)
                                  [:, row + k, m * P:(m + 1) * P] for w in (whi, wlo))
                        xh, xl = (t[:, 2 * (g % 2) + k, halves[half]] for t in (pool_hi_buf, pool_lo_buf))
                        mmul(bank[u % 4][:, :], wl, xh, start=k == 0, stop=False)
                        mmul(bank[u % 4][:, :], wh, xl, start=False, stop=False)
                        last = mmul(bank[u % 4][:, :], wh, xh, start=False, stop=k == 1)
                    last.then_inc(s.unit_done, 1)

        pe.wait_ge(s.consts, N_CONSTS)
        pe.wait_ge(s.gains_ready, 1)
        for g in range(GROUPS):
            pool_block(2 * g)
            pool_block(2 * g + 1)
            if g:
                pool_products(g - 1)
        pool_products(GROUPS - 1)

        def tile_products(n, par, hi, lo, nb=KD, ready=None, after_half=None):
            pe.wait_ge(s.w_ready, n + 1)
            for half in range(2):
                b = bank[2 * par + half]
                pe.wait_ge(s.unit_read, 2 * n + (unit(0, half) - 3))
                for k in range(nb):
                    if ready is not None:
                        ready(k, half)
                    xh, xl = hi[:, k, halves[half]], lo[:, k, halves[half]]
                    mmul(b[:, :], wlo[par][:, k, :], xh, start=k == 0, stop=False)
                    mmul(b[:, :], whi[par][:, k, :], xl, start=False, stop=False)
                    last = mmul(b[:, :], whi[par][:, k, :], xh, start=False, stop=k == nb - 1)
                last.then_inc(s.unit_done, 1)
                if after_half is not None:
                    after_half(half)

        def pairs(n0, start, end, *args, **kw):
            with pe.Fori(start, end) as i:
                for part in range(2):
                    tile_products(2 * i + (n0 + part), (n0 + part) % 2, *args, **kw)

        def x_blocks(index):
            return lambda k, half: pe.wait_ge(s.x_ready, 2 * (KD * index + k) + half + 1)

        def ffn(stage, x_index):
            l, n0, j0, nb, first, _ = stage
            if first:
                tile_products(n0, n0 % 2, x_hi_of[l], x_lo_of[l], ready=x_blocks(x_index),
                              after_half=lambda half: stats(x_index) if half == 0 else None)
                tile_products(n0 + 1, (n0 + 1) % 2, x_hi_of[l], x_lo_of[l])
            pairs(n0, int(first), nb, x_hi_of[l], x_lo_of[l])
            j_all = l * NJ + j0
            pairs(n0 + 2 * nb, 0, KD // 2, a_hi[l], a_lo[l], nb,
                  ready=lambda k, half: pe.wait_ge(s.a_ready, 2 * (j_all + k) + half + 1))

        for st in ffn_stages[:3]:
            ffn(st, 0)

        tile_products(T_GATE, T_GATE % 2, xhi, xlo, ready=x_blocks(1),
                      after_half=lambda half: stats(1) if half == 0 else None)
        pairs(T_QKV, 0, 8, xhi, xlo)
        pe.wait_ge(s.rows_final, 3)
        for kind, rows in enumerate((uu, ww, gi)):
            for c in range(NCH):
                at_col = (kind * NCH + c) * HEADS
                last = nc.tensor.transpose(bank[4][:, at_col:at_col + HEADS], rows[0:HEADS, c * CH:(c + 1) * CH],
                                           ident[0:HEADS, 0:HEADS])
        last.then_inc(s.cols_done, 1)
        pairs(T_O, 0, 4, xhi, xlo)

        def chunk_step(h, c):
            if chunk_ok(h, c, 0):
                i, p = h * NCH + c, c % 2
                pe.wait_ge(s.staged, i * 2 + (2 * SEED + 2))
                pe.wait_ge(s.s_ready, freed(i))
                pe.wait_ge(s.v_ready, freed(i))
                mmul(bank[6 + p][:, 0:CH], stage[:, p, 1, :], stage[:, p, 0, :], start=True, stop=True)
                for b in range(2):
                    last = nc.tensor.transpose(bank[6 + p][:, (b + 1) * CH:(b + 2) * CH], stage[:, p, 2 + b, :],
                                               ident[:, :])
                last.then_inc(s.st_done, 1)
                pe.wait_ge(s.kw_ready, freed(i))
                nc.tensor.transpose(bank[4 + p][:, 0:CH], stage[:, p, 1, :], ident[:, :]).then_inc(s.tr_done, 1)
            if chunk_ok(h, c, 1):
                _, cc, i = lagged(h, c, 1)
                p = cc % 2
                pe.wait_ge(s.s_ready, made(i))
                pe.wait_ge(s.v_ready, made(i))
                pe.wait_ge(s.hn_ready, freed(i))
                num = mmul(bank[p][:, 0:DV + 1], smat[:, p, :], kwv[:, p, CH:], start=True, stop=cc == 0)
                pe.wait_ge(s.kw_ready, made(i))
                pe.wait_ge(s.c_updated, i + SEED)
                pe.wait_ge(s.qs_ready, made(i))
                if cc:
                    num = mmul(bank[p][:, 0:DV + 1], qs[:, p, :], state[:, :], start=False, stop=True)
                num.then_inc(s.num_done, 1)
                mmul(bank[2][:, 0:DV + 1], kwv[:, p, 0:CH], kwv[:, p, CH:], start=True, stop=True) \
                    .then_inc(s.cupd_done, 1)
            if chunk_ok(h, c, 3):
                _, cc, i = lagged(h, c, 3)
                pe.wait_ge(s.hn_ready, made(i))
                pe.wait_ge(s.y_ready, i + SEED)
                for b in range(2):
                    last = nc.tensor.transpose(bank[3][:, b * CH:(b + 1) * CH],
                                               hn[:, cc % 2, b * CH:(b + 1) * CH], ident[:, :])
                last.then_inc(s.ht_done, 1)

        pe.wait_ge(s.unit_read, unit(T_O + 7, 1) + 1)
        pe.wait_ge(s.cols_ready, 1)
        for c in range(NCH):
            chunk_step(0, c)
        with pe.Fori(1, HEADS) as h:
            for c in range(NCH):
                chunk_step(h, c)
        for c in range(3):
            chunk_step(HEADS, c)

        pe.wait_ge(s.y_ready, SEED + HEADS * NCH)
        pe.wait_ge(s.c_updated, SEED + HEADS * NCH)
        pairs(T_OUT, 0, 4, xhi, xlo,
              ready=lambda k, half: pe.wait_ge(s.y_lo, SEED + (k // 2) * NCH + 4 * half + 4))

        for st in ffn_stages[3:]:
            ffn(st, 2)

        pe.wait_ge(s.acc_done, 2 * KD * 4)
        for t in range(KD):
            last = mmul(bank[4][:, t:t + 1], acc[:, t * P:(t + 1) * P], ones[:, 0:1], start=True, stop=True)
        last.then_inc(s.stat_done, 1)
        pe.wait_ge(s.fin_scaled, 2 * KD)
        pe.wait_ge(s.unit_read, unit(T_END - 1, 1) + 1)
        for t in range(KD):
            for part in range(2):
                k = 2 * t + part
                if t >= 2:
                    pe.wait_ge((s.ft_read_v, s.ft_read_a)[part], t - 1)
                for b in range(4):
                    last = nc.tensor.transpose(bank[k % 4][:, b * P:(b + 1) * P],
                                               x_fin[:, 4 * part + b, t * P:(t + 1) * P], ident[:, :])
                last.then_inc(s.ft_done, 1)

    @blk.scalar
    def _(act):
        fn = nc.scalar.activation

        def plain_wait():
            act.sem_inc(s.waits_passed, 1)

        def split_hi(n, par):
            act.wait_ge(raw_loaded[par], n * 8 + (16 - 8 * par))
            act.wait_ge(s.unit_done, n * 2 + (unit(0, 1) - 3))
            fn(whi[par][:, :, :], wraw[:, par, :, :], ACT.Copy).then_inc(s.w_hi, 1)

        def square(h, c, half, k):
            if not isinstance(k, int) or k >= 2:
                act.wait_ge(s.acc_done, k - 1)
            plain_wait()
            fn(blk3(sq[:, half, :]), one(h, c, halves[half]), ACT.Square).then_inc(s.sq_done, 1)

        def root(index):
            for half in range(2):
                act.wait_ge(s.var_ready, 2 * index + half + 1)
                fn(R[:, halves[half]], R[:, halves[half]], ACT.Sqrt).then_inc(s.sd_ready, 1)

        def high_of_x(h, c, half, gain_row, last=False, layer=0):
            plain_wait()
            fn(one(x_fin if last else x_hi_of[layer], c, halves[half]), one(h, c, halves[half]), ACT.Copy,
               scale=gain[:, gain_row, bass.ds(c, 1)]).then_inc(s.fin_scaled if last else s.x_hi, 1)

        for t in range(2):
            act.wait_ge(raw_loaded[t], 16)
            fn(whi[t][:, :, :], wraw[:, t, :, :], ACT.Copy).then_inc(s.w_hi, 1)
        for t in range(KD):
            act.wait_ge(x_loaded[t], 16)
            if t:
                act.wait_ge(s.x_ssq, t)
            fn(square_bin[:, :], x_tok[:, t, :], ACT.Square, accum_out=tok_stat[:, 0, t:t + 1]).then_inc(s.x_ssq, 1)
        act.wait_ge(s.gains_ready, 1)
        for g in range(GROUPS + 1):
            if g < GROUPS:
                if g >= 2:
                    act.wait_ge(s.unit_done, 4 * (g - 1))
                for c in (2 * g, 2 * g + 1):
                    for half in range(2):
                        k = 2 * c + half
                        act.wait_ge(s.pool_done, k + 1)
                        fn(pool_hi_buf[:, c % 4, halves[half]], bank[4 + k % 4][:, :], ACT.Copy,
                           scale=gain[:, G_POOL, c:c + 1]).then_inc(s.pool_hi, 1)
            if g == GROUPS - 1:
                act.wait_ge(s.unit_done, 8)
                act.wait_ge(raw_loaded[0], 32)
                fn(whi[0][:, :, :], wraw[:, 0, :, :], ACT.Copy).then_inc(s.w_hi, 1)
            if g:
                for c in (2 * g - 2, 2 * g - 1):
                    for half in range(2):
                        act.wait_ge(s.unit_read, 2 * c + half + 1)
                        high_of_x(h0, c, half, G_FFN0)
                        square(h0, c, half, 2 * c + half)

        def ffn_in_pair(stage, j, stat_index=None):
            l, n0 = stage[:2]
            n, par = j * 2 + n0, n0 % 2
            jj = (j + (l * NJ + stage[2])) * 2
            split_hi(n + 1, 1 - par)
            if stat_index is not None:
                root(stat_index)
            for half in range(2):
                act.wait_ge(s.unit_read, n * 2 + (unit(0, half) + 1))
                fn(gate_buf[:, half, :], gate_buf[:, half, :], ACT.Silu).then_inc(s.silu_done, 1)
            split_hi(n + 2, par)
            for half in range(2):
                act.wait_ge(s.unit_read, (n + 1) * 2 + (unit(0, half) + 1))
                plain_wait()
                fn(one(a_hi[l], j, halves[half]), blk3(act_buf[:, half, :]), ACT.Copy).then_inc(s.act_hi, 1)

        def out_pair(n0, i, h, completes, gain_row, sq0, final=False, last=False, spill=False):
            for part in range(2):
                n, par = i * 2 + (n0 + part), (n0 + part) % 2
                if not (last and part == 1):
                    split_hi(n + 1, 1 - par)
                if completes:
                    for half in range(2):
                        act.wait_ge(s.unit_read, n * 2 + (unit(0, half) + 1))
                        high_of_x(h, i * 2 + part, half, gain_row, final, int(h is h1))
                        square(h, i * 2 + part, half, i * 4 + (sq0 + 2 * part + half))
                    if spill:
                        act.dma_start(h_spill[:, bass.ds(i * 2 + part, 1), :], h[:, bass.ds(i * 2 + part, 1), :]) \
                           .then_inc(s.spilled, 16)

        def ffn(stage, stat_index, gain_row, sq0, final):
            l, n0, j0, nb, first, closes = stage
            if first:
                ffn_in_pair(stage, 0, stat_index)
            with act.Fori(int(first), nb) as j:
                ffn_in_pair(stage, j)
            final = final and closes
            with act.Fori(0, 3 if final else 4) as i:
                out_pair(n0 + 2 * nb, i, h_of[l], closes, gain_row, sq0, final, spill=closes and l == 0)
            if final:
                out_pair(n0 + 2 * nb, 3, h_of[l], closes, gain_row, sq0, final, last=True)

        for st in ffn_stages[:3]:
            ffn(st, 0, G_MLSTM, 2 * KD, False)

        split_hi(T_QKV, T_QKV % 2)
        root(1)
        act.wait_ge(s.bias_loaded, 32)
        act.wait_ge(s.unit_read, unit(T_GATE, 1) + 1)
        rows = slice(0, HEADS)
        fn(uu[rows, :], lf[rows, :], ACT.Abs, bias=bias_f[rows, :]).then_inc(s.gate_act, 1)
        fn(gi[rows, :], gi[rows, :], ACT.Identity, bias=bias_i[rows, :]).then_inc(s.gate_act, 1)
        act.wait_ge(s.gate_act, 1)
        fn(uu[rows, :], uu[rows, :], ACT.Exp, scale=-1.0).then_inc(s.gate_act, 1)
        act.wait_ge(s.gate_act, 3)
        fn(uu[rows, :], uu[rows, :], ACT.Ln, bias=1.0).then_inc(s.gate_act, 1)
        for n in range(T_QKV + 1, T_QKV + 5):
            split_hi(n, n % 2)
        act.wait_ge(s.gate_chain, GATE_STEPS)
        fn(ri[rows, 1, :], ri[rows, 1, :], ACT.Exp).then_inc(s.rows_final, 1)
        fn(ww[rows, :], ww[rows, :], ACT.Exp).then_inc(s.rows_final, 1)
        fn(gi[rows, :], mm[rows, :], ACT.Exp, scale=-1.0).then_inc(s.rows_final, 1)
        with act.Fori(2, 8) as i:
            for part in range(2):
                n0 = T_QKV + part
                split_hi(i * 2 + (n0 + 1), (n0 + 1) % 2)
        with act.Fori(0, 4) as i:
            for part in range(2):
                n0 = T_O + part
                split_hi(i * 2 + (n0 + 1), (n0 + 1) % 2)
                for half in range(2):
                    act.wait_ge(s.unit_read, i * 4 + (unit(n0, half) + 1))
                    fn(gate_buf[:, half, :], gate_buf[:, half, :], ACT.Sigmoid).then_inc(s.o_sig, 1)

        def chunk_step(h, c):
            if chunk_ok(h, c, 0):
                i, p = h * NCH + c, c % 2
                act.wait_ge(s.z_ready, made(i))
                fn(dmat[:, p, :], dmat[:, p, :], ACT.Exp).then_inc(s.d_ready, 1)
                act.wait_ge(s.tr_done, made(i))
                act.wait_ge(s.cupd_done, freed(i))
                plain_wait()
                fn(kwv[:, p, 0:CH], bank[4 + p][:, 0:CH], ACT.Copy, scale=cols[:, 1, c, bass.ds(h, 1)]) \
                    .then_inc(s.kw_ready, 1)
            if chunk_ok(h, c, 1):
                _, cc, i = lagged(h, c, 1)
                p = cc % 2
                act.wait_ge(s.num_done, made(i))
                act.wait_ge(s.rs_ready, freed(i))
                fn(tiny[:, p, 0:1], bank[p][:, DV:DV + 1], ACT.Abs).then_inc(s.den_ready, 1)
                act.wait_ge(s.ssq_ready, i + SEED)
                fn(core_bin[:, :], bank[p][:, 0:DV], ACT.Square, scale=DV ** -0.5, accum_out=tiny[:, p, 1:2]) \
                    .then_inc(s.ssq_ready, 1)
            if chunk_ok(h, c, 2):
                _, cc, i = lagged(h, c, 2)
                p = cc % 2
                act.wait_ge(s.rs_ready, made(i))
                act.wait_ge(s.ht_done, freed(i))
                fn(hn[:, p, :], bank[p][:, 0:DV], ACT.Copy, scale=tiny[:, p, 6:7]).then_inc(s.hn_ready, 1)
            if chunk_ok(h, c, 3):
                hh, cc, i = lagged(h, c, 3)
                act.wait_ge(s.y_ready, made(i))
                plain_wait()
                fn(xhi[:, bass.ds(hh * 2, 2), cc * CH:(cc + 1) * CH], yt[:, cc % 2, :, :], ACT.Copy) \
                    .then_inc(s.y_hi, 1)

        act.wait_ge(s.cols_ready, 1)
        act.wait_ge(s.core_consts, 2)
        act.wait_ge(s.unit_done, unit(T_O + 7, 1) + 1)
        for c in range(NCH):
            chunk_step(0, c)
        with act.Fori(1, HEADS) as h:
            for c in range(NCH):
                chunk_step(h, c)
        for c in range(3):
            chunk_step(HEADS, c)

        act.wait_ge(s.acc_zeroed, 4)
        with act.Fori(0, 4) as i:
            out_pair(T_OUT, i, h1, True, G_FFN1, 2 * KD * 2)
        for st in ffn_stages[3:]:
            ffn(st, 2, G_FINAL, 2 * KD * 3, True)

        act.wait_ge(s.var_tok, 1)
        fn(rstd_tok[:, :], rstd_tok[:, :], ACT.Sqrt).then_inc(s.sd_tok, 1)
        act.wait_ge(s.rstd_tok_ready, 1)
        for t in range(KD):
            act.wait_ge(s.ft_done, 2 * t + 2)
            if t >= 2:
                act.wait_ge(out_stored[t % 2], 16 * (t // 2))
            fn(out_rows[:, t % 2, HALF:], bank[(2 * t + 1) % 4][:, :], ACT.Copy, scale=rstd_tok[:, t:t + 1]) \
                .then_inc(s.ft_read_a, 1)

    @blk.vector
    def _(dve):
        v = nc.vector

        def split_lo(n, par):
            dve.wait_ge(s.w_hi, n + 1)
            v.tensor_tensor(wlo[par][:, :, :], wraw[:, par, :, :], whi[par][:, :, :].bitcast(F32), ALU.subtract) \
             .then_inc(s.w_ready, 1)

        def add_square(half, k):
            dve.wait_ge(s.sq_done, k + 1)
            if not isinstance(k, int) or k >= 2:
                dve.wait_ge(s.acc_done, k - 1)
            v.tensor_tensor(acc[:, halves[half]], acc[:, halves[half]], sq[:, half, :], ALU.add) \
             .then_inc(s.acc_done, 1)

        def rstd(index):
            for half in range(2):
                dve.wait_ge(s.stat_done, 2 * index + half + 1)
                v.tensor_scalar(R[:, halves[half]], bank[4 + half][:, :], 1.0 / D, EPS, ALU.mult, ALU.add) \
                 .then_inc(s.var_ready, 1)
            for half in range(2):
                dve.wait_ge(s.sd_ready, 2 * index + half + 1)
                v.reciprocal(R[:, halves[half]], R[:, halves[half]]).then_inc(s.rstd_ready, 1)
            v.memset(acc[:, :], 0.0).then_inc(s.acc_zeroed, 1)
            dve.wait_ge(s.rstd_ready, 2 * index + 2)
            dve.wait_ge(s.acc_zeroed, index + 2 + (index > 1))

        v.memset(acc[:, :], 0.0).then_inc(s.acc_zeroed, 1)
        split_lo(0, 0)
        split_lo(1, 1)
        for t in range(KD):
            dve.wait_ge(s.x_ssq, t + 1)
            v.tensor_scalar(tok_stat[:, 0, t:t + 1], tok_stat[:, 0, t:t + 1], 1.0 / D, EPS, ALU.mult, ALU.add) \
             .then_inc(s.x_var, 1)
            for part in range(2):
                k = 2 * t + part
                dve.wait_ge(s.xt_done, k + 1)
                v.tensor_copy(h0[:, 4 * part:4 * part + 4, t * P:(t + 1) * P],
                              bank[k % 4][:, :].rearrange("p (a b) -> p a b", a=4)).then_inc(s.xt_read, 1)
            dve.wait_ge(s.x_rstd, t + 1)
            v.tensor_scalar(x_tok[:, t, :], x_tok[:, t, :], tok_stat[:, 1, t:t + 1], None, ALU.mult) \
             .then_inc(s.xs_ready, 1)
        dve.wait_ge(s.gains_t, 1)
        v.tensor_copy(gain[:, :, :].rearrange("p a b -> p (a b)"), bank[7][:, 0:56]).then_inc(s.gains_ready, 1)
        dve.wait_ge(s.gains_ready, 1)
        dve.wait_ge(s.xt_read, 2 * KD)
        dve.wait_ge(s.acc_zeroed, 1)

        def low_of_x(h, c, half, gain_row, k, layer=0):
            dve.wait_ge(s.x_hi, k + 1)
            v.scalar_tensor_tensor(one(x_lo_of[layer], c, halves[half]), one(h, c, halves[half]),
                                   gain[:, gain_row, bass.ds(c, 1)],
                                   one(x_hi_of[layer], c, halves[half]).bitcast(F32), ALU.mult, ALU.subtract) \
             .then_inc(s.x_ready, 1)

        for g in range(GROUPS + 1):
            if g < GROUPS:
                for c in (2 * g, 2 * g + 1):
                    for half in range(2):
                        k = 2 * c + half
                        dve.wait_ge(s.pool_hi, k + 1)
                        v.scalar_tensor_tensor(pool_lo_buf[:, c % 4, halves[half]], bank[4 + k % 4][:, :],
                                               gain[:, G_POOL, c:c + 1],
                                               pool_hi_buf[:, c % 4, halves[half]].bitcast(F32),
                                               ALU.mult, ALU.subtract).then_inc(s.pool_ready, 1)
            if g == GROUPS - 1:
                split_lo(T_FFN0, 0)
            if g:
                for c in (2 * g - 2, 2 * g - 1):
                    for half in range(2):
                        u = 2 * c + half
                        dve.wait_ge(s.unit_done, u + 1)
                        hv = h0[:, c, halves[half]]
                        v.scalar_tensor_tensor(hv, bank[u % 4][:, :], gain[:, G_SCALE, c:c + 1], hv,
                                               ALU.mult, ALU.add).then_inc(s.unit_read, 1)
                        dve.wait_ge(s.unit_read, u + 1)
                        low_of_x(h0, c, half, G_FFN0, u)
                        add_square(half, u)

        def unit_bank(n0, half):
            return bank[2 * (n0 % 2) + half]

        def ffn_in_pair(stage, j, stat_index=None):
            l, n0 = stage[:2]
            n, par = j * 2 + n0, n0 % 2
            jj = (j + (l * NJ + stage[2])) * 2
            split_lo(n + 1, 1 - par)
            if stat_index is not None:
                rstd(stat_index)
            for half in range(2):
                dve.wait_ge(s.unit_done, n * 2 + (unit(0, half) + 1))
                v.tensor_tensor(gate_buf[:, half, :], bank[2 * par + half][:, :], R[:, halves[half]], ALU.mult) \
                 .then_inc(s.unit_read, 1)
            split_lo(n + 2, par)
            for half in range(2):
                dve.wait_ge(s.silu_done, jj + (half + 1))
                v.tensor_tensor(gate_buf[:, half, :], gate_buf[:, half, :], R[:, halves[half]], ALU.mult) \
                 .then_inc(s.silu_scaled, 1)
            for half in range(2):
                dve.wait_ge(s.unit_done, (n + 1) * 2 + (unit(0, half) + 1))
                dve.wait_ge(s.silu_scaled, jj + (half + 1))
                v.tensor_tensor(act_buf[:, half, :], bank[2 * (1 - par) + half][:, :], gate_buf[:, half, :],
                                ALU.mult).then_inc(s.unit_read, 1)
                dve.wait_ge(s.act_hi, jj + (half + 1))
                v.tensor_tensor(one(a_lo[l], j, halves[half]), blk3(act_buf[:, half, :]),
                                one(a_hi[l], j, halves[half]).bitcast(F32), ALU.subtract).then_inc(s.a_ready, 1)

        def out_pair(n0, i, h, completes, gain_row, x0, sq0, final=False, last=False):
            for part in range(2):
                n, par = i * 2 + (n0 + part), (n0 + part) % 2
                c = i * 2 + part
                if not (last and part == 1):
                    split_lo(n + 1, 1 - par)
                for half in range(2):
                    dve.wait_ge(s.unit_done, n * 2 + (unit(0, half) + 1))
                    v.tensor_tensor(one(h, c, halves[half]), blk3(bank[2 * par + half][:, :]),
                                    one(h, c, halves[half]), ALU.add).then_inc(s.unit_read, 1)
                    if completes:
                        dve.wait_ge(s.unit_read, n * 2 + (unit(0, half) + 1))
                        if not final:
                            low_of_x(h, c, half, gain_row, i * 4 + (x0 + 2 * part + half), int(h is h1))
                        add_square(half, i * 4 + (sq0 + 2 * part + half))

        def ffn(stage, stat_index, gain_row, x0, sq0, final):
            l, n0, j0, nb, first, closes = stage
            if first:
                ffn_in_pair(stage, 0, stat_index)
            with dve.Fori(int(first), nb) as j:
                ffn_in_pair(stage, j)
            final = final and closes
            with dve.Fori(0, 3 if final else 4) as i:
                out_pair(n0 + 2 * nb, i, h_of[l], closes, gain_row, x0, sq0, final)
            if final:
                out_pair(n0 + 2 * nb, 3, h_of[l], closes, gain_row, x0, sq0, final, last=True)

        for st in ffn_stages[:3]:
            ffn(st, 0, G_MLSTM, 2 * KD, 2 * KD, False)

        split_lo(T_QKV, T_QKV % 2)
        rstd(1)
        rows = slice(0, HEADS)
        dve.wait_ge(s.spilled, 16 * KD)
        b_gate = [bank[2 * (T_GATE % 2) + half] for half in range(2)]
        for half in range(2):
            hs = halves[half]
            dve.wait_ge(s.unit_done, unit(T_GATE, half) + 1)
            v.tensor_tensor(gi[rows, hs], b_gate[half][0:HEADS, :], R[0:HEADS, hs], ALU.mult)
            v.tensor_tensor(lf[rows, hs], b_gate[half][32:32 + HEADS, :], R[32:32 + HEADS, hs], ALU.mult) \
             .then_inc(s.unit_read, 1)
        gsteps = [0]

        def glink(ins):
            gsteps[0] += 1
            ins.then_inc(s.gate_chain, 1)
            dve.wait_ge(s.gate_chain, gsteps[0])

        def by_chunk(ap):
            return ap.rearrange("p (c t) -> p c t", t=CH)

        def gates_log():
            dve.wait_ge(s.gate_act, 1)
            dve.wait_ge(s.bias_loaded, 32)
            glink(v.tensor_scalar(lf[rows, :], lf[rows, :], bias_f[rows, :], 0.0, ALU.add, ALU.min))
            dve.wait_ge(s.gate_act, 4)
            glink(v.tensor_tensor(lf[rows, :], lf[rows, :], uu[rows, :], ALU.subtract))
            glink(v.memset(ww[rows, :], 1.0))
            glink(v.memset(by_chunk(ww[rows, :])[:, :, 0:1], 0.0))

        def gates_scan():
            glink(v.tensor_tensor_scan(bb[rows, :], ww[rows, :], lf[rows, :], 0.0, ALU.mult, ALU.add))
            glink(v.tensor_tensor_scan(mm[rows, :], lf[rows, :], gi[rows, :], 0.0, ALU.add, ALU.max))

        def gates_rows():
            glink(v.tensor_tensor(ri[rows, 0, :], bb[rows, :], mm[rows, :], ALU.subtract))
            glink(v.tensor_tensor(uu[rows, :], gi[rows, :], bb[rows, :], ALU.subtract))
            glink(v.memset(m_prev[rows, 0:1], 0.0))
            glink(v.tensor_copy(m_prev[rows, 1:NCH], by_chunk(mm[rows, :])[:, 0:NCH - 1, CH - 1]))

        def gates_logs():
            glink(v.tensor_tensor(by_chunk(ri[rows, 1, :]), by_chunk(ri[rows, 0, :]),
                                  m_prev[rows, :].rearrange("p (c a) -> p c a", a=1)
                                  .to_broadcast([HEADS, NCH, CH]), ALU.add))
            glink(v.tensor_tensor(by_chunk(ww[rows, :]), by_chunk(uu[rows, :]),
                                  by_chunk(ri[rows, 0, :])[:, :, CH - 1:CH].to_broadcast([HEADS, NCH, CH]),
                                  ALU.add))

        def qkv_tile(i, part, gate_part=None):
            n0 = T_QKV + part
            split_lo(i * 2 + (n0 + 1), (n0 + 1) % 2)
            if gate_part is not None:
                gate_part()
            for half in range(2):
                dve.wait_ge(s.unit_done, i * 4 + (unit(n0, half) + 1))
                v.tensor_tensor(one(qkv, i * 2 + part, halves[half]), blk3(unit_bank(n0, half)[:, :]),
                                blk3(R[:, halves[half]]), ALU.mult).then_inc(s.unit_read, 1)

        qkv_tile(0, 0, gates_log)
        qkv_tile(0, 1, gates_scan)
        qkv_tile(1, 0, gates_rows)
        qkv_tile(1, 1, gates_logs)
        assert gsteps[0] == GATE_STEPS
        with dve.Fori(2, 8) as i:
            for part in range(2):
                qkv_tile(i, part)
        dve.wait_ge(s.cols_done, 1)
        v.tensor_copy(cols[:, :, :, :].rearrange("p a b c -> p (a b c)"), bank[4][:, 0:3 * NCH * HEADS]) \
         .then_inc(s.cols_ready, 1)
        dve.wait_ge(s.rows_out, 16)
        with dve.Fori(0, 4) as i:
            for part in range(2):
                n0 = T_O + part
                split_lo(i * 2 + (n0 + 1), (n0 + 1) % 2)
                for half in range(2):
                    dve.wait_ge(s.unit_done, i * 4 + (unit(n0, half) + 1))
                    v.tensor_tensor(gate_buf[:, half, :], unit_bank(n0, half)[:, :], R[:, halves[half]], ALU.mult) \
                     .then_inc(s.unit_read, 1)
                    dve.wait_ge(s.o_sig, i * 4 + (2 * part + half + 1))
                    v.tensor_scalar(one(sig_o, i * 2 + part, halves[half]), blk3(gate_buf[:, half, :]),
                                    gain[:, G_HEAD, bass.ds(i * 2 + part, 1)], None, ALU.mult) \
                     .then_inc(s.o_ready, 1)

        def chunk_step(h, c):
            if chunk_ok(h, c, 0):
                i, p = h * NCH + c, c % 2
                dve.wait_ge(bc_loaded[c % 4], h * 32 + 16 * (c // 4 + 1))
                v.scalar_tensor_tensor(dmat[:, p, :], bc[:, c % 4, 0, :], cols[:, 0, c, bass.ds(h, 1)],
                                       causal[:, :], ALU.add, ALU.add).then_inc(s.z_ready, 1)
                dve.wait_ge(s.staged, i * 2 + (2 * SEED + 2))
                dve.wait_ge(s.num_done, freed(i))
                v.scalar_tensor_tensor(qs[:, p, :], stage[:, p, 0, :], QSCALE, bc[:, c % 4, 1, :],
                                       ALU.mult, ALU.mult).then_inc(s.qs_ready, 1)
                dve.wait_ge(s.st_done, made(i))
                dve.wait_ge(s.cupd_done, freed(i))
                v.tensor_copy(kwv[:, p, CH:CH + DV], bank[6 + p][:, CH:CH + DV]).then_inc(s.v_ready, 1)
            if chunk_ok(h, c, 1):
                _, cc, i = lagged(h, c, 1)
                dve.wait_ge(s.cupd_done, made(i))
                dve.wait_ge(s.c_updated, i + SEED)
                if cc:
                    v.scalar_tensor_tensor(state[:, :], state[:, :], bc[:, cc % 4, 1, CH - 1:CH],
                                           bank[2][:, 0:DV + 1], ALU.mult, ALU.add).then_inc(s.c_updated, 1)
                else:
                    v.tensor_copy(state[:, :], bank[2][:, 0:DV + 1]).then_inc(s.c_updated, 1)
            if chunk_ok(h, c, 0):
                i, p = h * NCH + c, c % 2
                dve.wait_ge(s.d_ready, made(i))
                v.scalar_tensor_tensor(smat[:, p, :], bank[6 + p][:, 0:CH], QSCALE, dmat[:, p, :],
                                       ALU.mult, ALU.mult).then_inc(s.s_ready, 1)
            if chunk_ok(h, c, 3):
                hh, cc, i = lagged(h, c, 3)
                dve.wait_ge(s.ht_done, made(i))
                dve.wait_ge(s.y_lo, freed(i))
                v.tensor_tensor(yt[:, cc % 2, :, :], bank[3][:, 0:DV].rearrange("p (a t) -> p a t", a=2),
                                sig_o[:, bass.ds(hh * 2, 2), cc * CH:(cc + 1) * CH], ALU.mult) \
                 .then_inc(s.y_ready, 1)
            if chunk_ok(h, c, 4):
                hh, cc, i = lagged(h, c, 4)
                tok = slice(cc * CH, (cc + 1) * CH)
                dve.wait_ge(s.y_hi, made(i))
                v.tensor_tensor(xlo[:, bass.ds(hh * 2, 2), tok], yt[:, cc % 2, :, :],
                                xhi[:, bass.ds(hh * 2, 2), tok].bitcast(F32), ALU.subtract).then_inc(s.y_lo, 1)

        dve.wait_ge(s.cols_ready, 1)
        dve.wait_ge(s.o_ready, 16)
        for c in range(NCH):
            chunk_step(0, c)
        with dve.Fori(1, HEADS) as h:
            for c in range(NCH):
                chunk_step(h, c)
        for c in range(4):
            chunk_step(HEADS, c)

        dve.wait_ge(s.y_hi, SEED + HEADS * NCH)
        dve.wait_ge(s.y_lo, SEED + HEADS * NCH)
        v.memset(acc[:, :], 0.0).then_inc(s.acc_zeroed, 1)
        dve.wait_ge(s.acc_zeroed, 4)
        dve.wait_ge(s.h_back, 16)
        with dve.Fori(0, 4) as i:
            out_pair(T_OUT, i, h1, True, G_FFN1, 2 * KD * 2, 2 * KD * 2)
        for st in ffn_stages[3:]:
            ffn(st, 2, G_FINAL, None, 2 * KD * 3, True)

        dve.wait_ge(s.stat_done, 7)
        v.tensor_scalar(rstd_tok[:, :], bank[4][:, 0:KD], 1.0 / D, EPS, ALU.mult, ALU.add).then_inc(s.var_tok, 1)
        dve.wait_ge(s.sd_tok, 1)
        v.reciprocal(rstd_tok[:, :], rstd_tok[:, :]).then_inc(s.rstd_tok_ready, 1)
        dve.wait_ge(s.rstd_tok_ready, 1)
        for t in range(KD):
            dve.wait_ge(s.ft_done, 2 * t + 1)
            if t >= 2:
                dve.wait_ge(out_stored[t % 2], 16 * (t // 2))
            v.tensor_scalar(out_rows[:, t % 2, 0:HALF], bank[(2 * t) % 4][:, :], rstd_tok[:, t:t + 1], None,
                            ALU.mult).then_inc(s.ft_read_v, 1)

    block.__exit__(None, None, None)


_INS = ["x", "pool_norm", "pool_w", "pool_scale", "mlstm_norm", "mlstm_w_in", "mlstm_gate_bias",
        "mlstm_head_norm", "mlstm_w_out", "ffn_norm", "ffn_w_in", "ffn_w_out", "final_norm"]
_OUTS = [((1, NT, D), "float32")]


def kernel(**inputs):
    import numpy as _np
    import concourse.bacc as _bacc
    from concourse import mybir as _mybir
    from concourse.bass_utils import run_bass_kernel_spmd as _run

    nc = _bacc.Bacc("TRN2", target_bir_lowering=False, num_devices=1)
    arrays, args = {}, []
    for name in _INS:
        a = _np.ascontiguousarray(inputs[name])
        arrays[f"in_{name}_dram"] = a
        args.append(nc.dram_tensor(f"in_{name}_dram", a.shape, _mybir.dt.from_np(a.dtype), kind="ExternalInput").ap())
    for i, (shape, dtype) in enumerate(_OUTS):
        dt = _mybir.dt.from_np(_np.dtype(dtype))
        args.append(nc.dram_tensor(f"out_{i}_dram", shape, dt, kind="ExternalOutput").ap())
    build(nc, *args)
    r = _run(nc, [arrays], core_ids=[0])
    got = tuple(r.results[0][f"out_{i}_dram"] for i in range(len(_OUTS)))
    return got[0]
```

```python
import concourse.bass as bass
from concourse import mybir
from concourse.alu_op_type import AluOpType as ALU

F32 = mybir.dt.float32
F32R = mybir.dt.float32r
ACT = mybir.ActivationFunctionType

P = 128
D = 1024
NT = 1024
HALF = 512
KD = D // P
D_FF = 2816
NJ = D_FF // P
FFN_BLOCKS = [(0, 8), (8, 7), (15, 7)]
HEADS = 4
DQK = 128
DV = 256
QSCALE = DQK ** -0.5
CH = 128
NCH = NT // CH
EPS = 1e-6
TINY = 2.0e-38
NEG = -3.0e38
GROUPS = 4
LONGEST = 16

T_FFN0 = 2
N_FFN = 2 * NJ + 3 * KD
T_GATE = T_FFN0 + N_FFN
T_QKV = T_GATE + 1
T_O = T_QKV + 16
T_OUT = T_O + 8
T_FFN1 = T_OUT + 8
T_END = T_FFN1 + N_FFN

G_POOL, G_SCALE, G_MLSTM, G_HEAD, G_FFN0, G_FFN1, G_FINAL = range(7)


def unit(n, half):
    return 2 * n + 12 + half


FINAL_ORDER = [(0, 0), (1, 0), (0, 1), (1, 1)]
FINAL_UNIT = unit(T_END - 2, 0)

SEED = 4
GATE_STEPS = 12
N_CONSTS = 5 + 6 * GROUPS


def lagged(h, c, lag):
    return (h, c - lag, h * NCH + (c - lag)) if c >= lag else (h - 1, c - lag + NCH, h * NCH + (c - lag))


def chunk_ok(h, c, lag):
    return not isinstance(h, int) or 0 <= h * NCH + c - lag < HEADS * NCH


class Semaphores:
    pass


def made(i):
    return i + (SEED + 1)


def freed(i):
    return i + (SEED - 1)


def build(nc, x, pool_norm, pool_w, pool_scale, mlstm_norm, mlstm_w_in, mlstm_gate_bias, mlstm_head_norm,
          mlstm_w_out, ffn_norm, ffn_w_in, ffn_w_out, final_norm, out):
    h_spill = nc.dram_tensor("h_spill", [P, KD, NT], F32, kind="Internal").ap()
    rows_dram = nc.dram_tensor("rows_dram", [HEADS, 2, NT], F32, kind="Internal").ap()

    base = (nc.sbuf_base + 31) // 32 * 32
    arena_bytes = 212768
    nc.alloc_sbuf_tensor("arena", [P, arena_bytes // 4], F32)
    cursor = [base]

    def at(name, shape, dt, offset=None):
        size = 4
        for s in shape[1:]:
            size *= s
        if offset is None:
            offset = cursor[0]
            cursor[0] += (size + 31) // 32 * 32
            assert cursor[0] <= base + arena_bytes, (name, cursor[0] - base)
        return nc.alloc_sbuf_tensor_at(name, shape, dt, offset=offset)

    o_xhi = base
    xhi = at("xhi", [P, KD, NT], F32R)
    o_xlo = cursor[0]
    xlo = at("xlo", [P, KD, NT], F32R)
    o_b = cursor[0]
    cursor[0] += 3 * 32768
    wraw = at("wraw", [P, 2, KD, P], F32)
    whi = [at(f"whi{s}", [P, KD, P], F32R) for s in range(2)]
    wlo = [at(f"wlo{s}", [P, KD, P], F32R) for s in range(2)]
    ident = at("ident", [P, P], F32)
    ones = at("ones", [P, P], F32)
    causal = at("causal", [P, P], F32)
    gain = at("gain", [P, 7, KD], F32)
    bias_i = at("bias_i", [P, 1], F32)
    bias_f = at("bias_f", [P, 1], F32)
    minus_half = at("minus_half", [P, 1], F32)
    cols = at("cols", [P, 3, NCH, HEADS], F32)
    m_prev = at("m_prev", [P, NCH], F32)
    rstd_tok = at("rstd_tok", [P, KD], F32)
    o_tmp = cursor[0]
    R = at("R", [P, NT], F32)
    gate_buf = at("gate_buf", [P, 2, HALF], F32)
    act_buf = at("act_buf", [P, 2, HALF], F32)
    sq = at("sq", [P, 2, HALF], F32)
    acc = at("acc", [P, NT], F32)

    h0 = at("h0", [P, KD, NT], F32, o_b + 65536)
    x_hi_of = [xhi, at("x_hi1", [P, KD, NT], F32R, o_b + 32768)]
    x_lo_of = [xlo, at("x_lo1", [P, KD, NT], F32R, o_b + 65536)]
    a_hi = [at("a_hi0", [P, KD, NT], F32R, o_b), xhi]
    a_lo = [at("a_lo0", [P, KD, NT], F32R, o_b + 32768), xlo]
    h1 = at("h1", [P, KD, NT], F32, o_b)
    qkv = at("qkv", [P, 16, NT], F32, o_b)
    sig_o = at("sig_o", [P, KD, NT], F32, o_b + 65536)
    gi = at("gi", [P, NT], F32, o_b + 65536)
    lf = at("lf", [P, NT], F32, o_b + 65536 + 4096)
    bb = at("bb", [P, NT], F32, o_b + 65536 + 8192)
    mm = at("mm", [P, NT], F32, o_b + 65536 + 12288)
    ri = at("ri", [P, 2, NT], F32, o_b + 65536 + 16384)
    uu = at("uu", [P, NT], F32, o_b + 65536 + 24576)
    ww = at("ww", [P, NT], F32, o_b + 65536 + 28672)
    x_tok = at("x_tok", [P, KD, D], F32, o_b + 32768)
    pool_hi_buf = at("pool_hi_buf", [P, 4, NT], F32R, o_b)
    pool_lo_buf = at("pool_lo_buf", [P, 4, NT], F32R, o_b + 16384)
    gain_rows = at("gain_rows", [P, P], F32, o_tmp)
    inv_count = at("inv_count", [P, LONGEST], F32, o_tmp + 512)
    win_main = at("win_main", [P, GROUPS, P + LONGEST], F32, o_tmp + 4096)
    win_first = at("win_first", [P, GROUPS, P + LONGEST], F32, o_tmp + 6400)
    tok_stat = at("tok_stat", [P, 2, KD], F32, o_tmp + 8704)
    zero_row = at("zero_row", [P, HALF], F32R, o_tmp + 9216)
    square_bin = at("square_bin", [P, D], F32, o_xlo)
    x_fin = at("x_fin", [P, KD, NT], F32, o_b + 32768)
    out_rows = at("out_rows", [P, KD, D], F32, o_b + 65536)
    cursor_core = [o_tmp]

    def core(name, shape):
        t = at(name, shape, F32, cursor_core[0])
        size = 4
        for s in shape[1:]:
            size *= s
        cursor_core[0] += (size + 31) // 32 * 32
        assert cursor_core[0] <= base + arena_bytes
        return t

    kwv = core("kwv", [P, 2, CH + DV + 1])
    dmat = core("dmat", [P, 2, CH])
    smat = core("smat", [P, 2, CH])
    qs = core("qs", [P, 2, CH])
    state = core("state", [P, DV + 1])
    tiny = core("tiny", [P, 2, 5])
    cursor_core[0] = o_tmp + 8192
    bc = core("bc", [P, 4, 2, CH])
    stage = core("stage", [P, 2, 4, CH])
    hn = core("hn", [P, 2, DV])
    yt = core("yt", [P, 2, 2, CH])
    core_bin = at("core_bin", [P, DV], F32, o_xlo + 4 * (KD * NT - DV))

    bank = [nc.alloc_psum_tensor(f"bank{i}", [P, HALF], F32) for i in range(8)]

    s = Semaphores()
    x_loaded = [nc.alloc_semaphore(f"x_loaded{t}") for t in range(KD)]
    s.gains_loaded = nc.alloc_semaphore("gains_loaded")
    s.bias_loaded = nc.alloc_semaphore("bias_loaded")
    s.gate_i_loaded = nc.alloc_semaphore("gate_i_loaded")
    s.raw_even = nc.alloc_semaphore("raw_even")
    s.raw_odd = nc.alloc_semaphore("raw_odd")
    s.w_hi = nc.alloc_semaphore("w_hi")
    s.w_ready = nc.alloc_semaphore("w_ready")
    s.unit_done = nc.alloc_semaphore("unit_done")
    s.unit_read = nc.alloc_semaphore("unit_read")
    s.consts = nc.alloc_semaphore("consts")
    s.gains_t = nc.alloc_semaphore("gains_t")
    s.gains_ready = nc.alloc_semaphore("gains_ready")
    s.xt_done = nc.alloc_semaphore("xt_done")
    s.xt_read = nc.alloc_semaphore("xt_read")
    s.x_ssq = nc.alloc_semaphore("x_ssq")
    s.x_var = nc.alloc_semaphore("x_var")
    s.x_rstd = nc.alloc_semaphore("x_rstd")
    s.xs_ready = nc.alloc_semaphore("xs_ready")
    s.pool_done = nc.alloc_semaphore("pool_done")
    s.sq_done = nc.alloc_semaphore("sq_done")
    s.acc_done = nc.alloc_semaphore("acc_done")
    s.acc_zeroed = nc.alloc_semaphore("acc_zeroed")
    s.stat_done = nc.alloc_semaphore("stat_done")
    s.var_ready = nc.alloc_semaphore("var_ready")
    s.sd_ready = nc.alloc_semaphore("sd_ready")
    s.rstd_ready = nc.alloc_semaphore("rstd_ready")
    s.pool_hi = nc.alloc_semaphore("pool_hi")
    s.pool_ready = nc.alloc_semaphore("pool_ready")
    s.x_hi = nc.alloc_semaphore("x_hi")
    s.x_ready = nc.alloc_semaphore("x_ready")
    s.silu_done = nc.alloc_semaphore("silu_done")
    s.silu_scaled = nc.alloc_semaphore("silu_scaled")
    s.act_hi = nc.alloc_semaphore("act_hi")
    s.a_ready = nc.alloc_semaphore("a_ready")
    s.spilled = nc.alloc_semaphore("spilled")
    s.h_back = nc.alloc_semaphore("h_back")
    s.rows_out = nc.alloc_semaphore("rows_out")
    s.gate_chain = nc.alloc_semaphore("gate_chain")
    s.gate_act = nc.alloc_semaphore("gate_act")
    s.rows_final = nc.alloc_semaphore("rows_final")
    s.cols_done = nc.alloc_semaphore("cols_done")
    s.cols_ready = nc.alloc_semaphore("cols_ready")
    s.o_sig = nc.alloc_semaphore("o_sig")
    s.o_ready = nc.alloc_semaphore("o_ready")
    s.staged = nc.alloc_semaphore("staged")
    s.v_staged = nc.alloc_semaphore("v_staged")
    s.tr_done = nc.alloc_semaphore("tr_done")
    s.kw_ready = nc.alloc_semaphore("kw_ready")
    s.v_ready = nc.alloc_semaphore("v_ready")
    s.floor_ready = nc.alloc_semaphore("floor_ready")
    s.var_made = nc.alloc_semaphore("var_made")
    s.den_ready = nc.alloc_semaphore("den_ready")
    s.cols_read = nc.alloc_semaphore("cols_read")
    s.bc0 = nc.alloc_semaphore("bc0")
    s.bc1 = nc.alloc_semaphore("bc1")
    s.bc2 = nc.alloc_semaphore("bc2")
    s.bc3 = nc.alloc_semaphore("bc3")
    s.z_ready = nc.alloc_semaphore("z_ready")
    s.d_ready = nc.alloc_semaphore("d_ready")
    s.st_done = nc.alloc_semaphore("st_done")
    s.s_ready = nc.alloc_semaphore("s_ready")
    s.qs_ready = nc.alloc_semaphore("qs_ready")
    s.num_done = nc.alloc_semaphore("num_done")
    s.cupd_done = nc.alloc_semaphore("cupd_done")
    s.c_updated = nc.alloc_semaphore("c_updated")
    s.ssq_ready = nc.alloc_semaphore("ssq_ready")
    s.rs_ready = nc.alloc_semaphore("rs_ready")
    s.hn_ready = nc.alloc_semaphore("hn_ready")
    s.ht_done = nc.alloc_semaphore("ht_done")
    s.y_ready = nc.alloc_semaphore("y_ready")
    s.y_hi = nc.alloc_semaphore("y_hi")
    s.y_lo = nc.alloc_semaphore("y_lo")
    s.core_consts = nc.alloc_semaphore("core_consts")
    s.waits_passed = nc.alloc_semaphore("waits_passed")
    s.fin_scaled = nc.alloc_semaphore("fin_scaled")
    s.var_tok = nc.alloc_semaphore("var_tok")
    s.sd_tok = nc.alloc_semaphore("sd_tok")
    s.rstd_tok_ready = nc.alloc_semaphore("rstd_tok_ready")
    s.ft_left = nc.alloc_semaphore("ft_left")
    s.ft_right = nc.alloc_semaphore("ft_right")
    s.ft_read_v = nc.alloc_semaphore("ft_read_v")
    s.ft_read_a = nc.alloc_semaphore("ft_read_a")
    s.out_stored = nc.alloc_semaphore("out_stored")
    raw_loaded = [s.raw_even, s.raw_odd]
    bc_loaded = [s.bc0, s.bc1, s.bc2, s.bc3]
    halves = [slice(0, HALF), slice(HALF, NT)]

    def pool_unit_bank(u):
        return bank[u % 4 + 4 * (u // 4 == GROUPS - 1)]

    def blk3(ap):
        return ap.rearrange("p (a n) -> p a n", a=1)

    def one(t, c, cols_):
        return t[:, bass.ds(c, 1), cols_]

    w_in_view = [ffn_w_in[l].rearrange("(k p) m -> p k m", p=P) for l in range(2)]
    w_out_view = [ffn_w_out[l].rearrange("(k p) m -> p k m", p=P) for l in range(2)]
    w_mix = mlstm_w_in[0].rearrange("(k p) m -> p k m", p=P)
    w_mix_out = mlstm_w_out[0].rearrange("(k p) m -> p k m", p=P)

    ffn_stages = []
    for l, n in ((0, T_FFN0), (1, T_FFN1)):
        for b, (j0, nb) in enumerate(FFN_BLOCKS):
            ffn_stages.append((l, n, j0, nb, b == 0, b == len(FFN_BLOCKS) - 1))
            n += 2 * nb + KD

    h_of = [h0, h1]
    block = nc.Block()
    blk = block.__enter__()

    @blk.sync
    def _(sp):
        for t in range(KD):
            sp.dma_start(x_tok[:, t, :], x[0, t * P:(t + 1) * P, :]).then_inc(x_loaded[t], 16)
        for r, g in enumerate([pool_norm[0], pool_scale[0], mlstm_norm[0], mlstm_head_norm[0], ffn_norm[0],
                               ffn_norm[1], final_norm]):
            sp.dma_start(gain_rows[r * KD:(r + 1) * KD, :], g.rearrange("(k p) -> k p", p=P)) \
              .then_inc(s.gains_loaded, 16)
        with nc.allow_non_contiguous_dma(reason="eight biases, one per partition"):
            for bias, h in ((bias_i, 0), (bias_f, HEADS)):
                sp.dma_start(bias[0:HEADS, :], mlstm_gate_bias[0, h:h + HEADS].rearrange("(h a) -> h a", a=1)) \
                  .then_inc(s.bias_loaded, 16)
        for t in range(2):
            sp.dma_start(wraw[:, t, :, :].rearrange("p (a b) m -> p a (b m)", b=2),
                         pool_w[0, 2 * t:2 * t + 2].rearrange("g (k p) m -> p (g k) m", p=P)) \
              .then_inc(raw_loaded[t], 16)

        def load(n, par, src, nb=KD):
            sp.wait_ge(s.w_ready, n - 1)
            sp.dma_start(wraw[:, par, 0:nb, :], src).then_inc(raw_loaded[par], 16)

        def ffn_loads(stage):
            l, n0, j0, nb, _, _ = stage
            with sp.Fori(0, nb) as j:
                for part in range(2):
                    load(n0 + part + 2 * j, (n0 + part) % 2,
                         w_in_view[l][:, :, bass.ds(j * P + (part * D_FF + j0 * P), P)])
            with sp.Fori(0, KD // 2) as c:
                for part in range(2):
                    load(n0 + 2 * nb + part + 2 * c, (n0 + part) % 2,
                         w_out_view[l][:, j0:j0 + nb, bass.ds(c * (2 * P) + part * P, P)], nb)

        for st in ffn_stages[:3]:
            ffn_loads(st)
        sp.wait_ge(s.w_ready, T_GATE - 1)
        gate_cols = 2 * HEADS * DQK + 2 * HEADS * DV
        sp.dma_start(wraw[:, T_GATE % 2, :, 0:HEADS], w_mix[:, :, gate_cols:gate_cols + HEADS]) \
          .then_inc(s.gate_i_loaded, 16)
        sp.wait_ge(s.gate_i_loaded, 16)
        sp.dma_start(wraw[:, T_GATE % 2, :, 32:32 + HEADS], w_mix[:, :, gate_cols + HEADS:gate_cols + 2 * HEADS]) \
          .then_inc(raw_loaded[T_GATE % 2], 16)

        def mix_loads(n0, c0, count):
            with sp.Fori(0, count // 2) as c:
                for part in range(2):
                    load(n0 + part + 2 * c, (n0 + part) % 2,
                         w_mix[:, :, bass.ds(c * (2 * P) + (c0 + part) * P, P)])

        mix_loads(T_QKV, 0, 16)
        sp.wait_ge(s.rows_final, 3)
        sp.dma_start(rows_dram, ri[0:HEADS, :, :]).then_inc(s.rows_out, 16)
        mix_loads(T_O, 16, 8)
        load(T_OUT, T_OUT % 2, w_mix_out[:, :, 0:P])
        sp.wait_ge(s.rows_out, 16)
        sp.wait_ge(s.acc_zeroed, 3)
        with sp.Fori(0, HEADS) as h:
            for c in range(NCH):
                sp.wait_ge(s.c_updated, h * NCH + (c + 1))
                sp.dma_start(bc[:, c % 4, :, :],
                             rows_dram[bass.ds(h, 1), :, c * CH:(c + 1) * CH].to_broadcast([P, 2, CH])) \
                  .then_inc(bc_loaded[c % 4], 16)
        sp.wait_ge(s.staged, SEED + HEADS * NCH)
        sp.wait_ge(s.v_staged, SEED + HEADS * NCH)
        sp.wait_ge(s.spilled, 16 * KD)
        sp.dma_start(h1[:, :, :], h_spill).then_inc(s.h_back, 16)
        load(T_OUT + 1, (T_OUT + 1) % 2, w_mix_out[:, :, P:2 * P])
        with sp.Fori(1, KD // 2) as c:
            for part in range(2):
                load(T_OUT + part + 2 * c, (T_OUT + part) % 2,
                     w_mix_out[:, :, bass.ds(c * (2 * P) + part * P, P)])
        for st in ffn_stages[3:]:
            ffn_loads(st)
        for t in range(KD):
            sp.wait_ge(s.ft_read_v, t + 1)
            sp.wait_ge(s.ft_read_a, t + 1)
            sp.dma_start(out[0, t * P:(t + 1) * P, :], out_rows[:, t, :]).then_inc(s.out_stored, 16)
        sp.wait_ge(s.out_stored, 16 * KD)

    @blk.gpsimd
    def _(pool):
        g = nc.gpsimd
        for sem in (s.tr_done, s.z_ready, s.d_ready, s.st_done, s.s_ready, s.qs_ready, s.num_done, s.kw_ready,
                    s.v_ready, s.cupd_done, s.c_updated, s.hn_ready, s.ht_done, s.y_ready, s.y_hi, s.y_lo, s.ssq_ready,
                    s.den_ready, s.floor_ready, s.var_made, s.rs_ready, s.staged, s.v_staged):
            pool.sem_inc(sem, SEED)
        g.memset(ident[:, :], 0.0).then_inc(s.consts, 1)
        g.memset(ones[:, :], 1.0).then_inc(s.consts, 1)
        g.memset(causal[:, :], 0.0).then_inc(s.consts, 1)
        pool.wait_ge(s.consts, 3)
        g.affine_select(out=ident[:, :], in_=ident[:, :], compare_op=ALU.not_equal, fill=1.0, base=0,
                        pattern=[[-1, P]], channel_multiplier=1).then_inc(s.consts, 1)
        g.affine_select(out=causal[:, :], in_=causal[:, :], compare_op=ALU.is_ge, fill=NEG, base=0,
                        pattern=[[1, P]], channel_multiplier=-1).then_inc(s.consts, 1)
        g.memset(minus_half[:, :], -0.5)
        g.memset(zero_row[0:1, :].bitcast(F32), 0.0)
        for t in range(LONGEST):
            g.memset(inv_count[:, t:t + 1], 1.0 / (t + 1))
        for gr in range(GROUPS):
            win = 2 << gr
            g.memset(win_main[:, gr, :], 1.0 / win)
            g.memset(win_first[:, gr, win:], 1.0 / win).then_inc(s.consts, 1)
        pool.wait_ge(s.consts, 5 + GROUPS)
        for gr in range(GROUPS):
            win = 2 << gr
            g.tensor_copy(win_first[:, gr, 0:win], inv_count[:, 0:win]).then_inc(s.consts, 1)
        pool.wait_ge(s.consts, 5 + 2 * GROUPS)
        for gr in range(GROUPS):
            for m in (win_main, win_first):
                last = g.affine_select(out=m[:, gr, :], in_=m[:, gr, :], compare_op=ALU.is_ge, fill=0.0, base=0,
                                       pattern=[[1, P + LONGEST]], channel_multiplier=-1)
            last.then_inc(s.consts, 1)
        pool.wait_ge(s.consts, 5 + 3 * GROUPS)
        for gr in range(GROUPS):
            win = 2 << gr
            for m in (win_main, win_first):
                last = g.affine_select(out=m[:, gr, :], in_=m[:, gr, :], compare_op=ALU.is_ge, fill=0.0,
                                       base=win - 1, pattern=[[-1, P + LONGEST]], channel_multiplier=1)
            last.then_inc(s.consts, 1)
        for t in range(KD):
            pool.wait_ge(s.x_var, t + 1)
            g.tensor_tensor(tok_stat[:, 1, t:t + 1], tok_stat[:, 0, t:t + 1], minus_half[:, :], ALU.pow) \
             .then_inc(s.x_rstd, 1)
        pool.wait_ge(s.acc_zeroed, 1)
        for k in range(2 * KD):
            half = k % 2
            pool.wait_ge(s.sq_done, k + 1)
            if k >= 2:
                pool.wait_ge(s.acc_done, k - 1)
            g.tensor_tensor(acc[:, halves[half]], acc[:, halves[half]], sq[:, half, :], ALU.add) \
             .then_inc(s.acc_done, 1)
        def chunk_step(h, c):
            if chunk_ok(h, c, 0):
                i, tok = h * NCH + c, slice(c * CH, (c + 1) * CH)
                pool.wait_ge(s.tr_done, freed(i))
                pool.wait_ge(s.qs_ready, freed(i))
                g.tensor_copy(stage[:, c % 2, 0:1, :], qkv[:, bass.ds(h, 1), tok])
                g.tensor_copy(stage[:, c % 2, 1:2, :], qkv[:, bass.ds(h + HEADS, 1), tok]).then_inc(s.staged, 1)
            if chunk_ok(h, c, 2):
                hh, cc, i = lagged(h, c, 2)
                ty = tiny[:, cc % 2, :]
                pool.wait_ge(s.var_made, freed(i))
                g.tensor_copy(ty[:, 4:5], cols[:, 2, cc, bass.ds(hh, 1)]).then_inc(s.floor_ready, 1)
                pool.wait_ge(s.floor_ready, made(i))
                pool.wait_ge(s.den_ready, made(i))
                pool.wait_ge(s.ssq_ready, made(i))
                pool.wait_ge(s.hn_ready, freed(i))
                pool.sem_inc(s.waits_passed, 1)
                g.tensor_scalar(ty[:, 2:3], ty[:, 0:1], ty[:, 4:5], ty[:, 1:2], ALU.max, ALU.add).then_inc(s.var_made, 1)
                pool.wait_ge(s.var_made, made(i))
                g.tensor_tensor(ty[:, 3:4], ty[:, 2:3], minus_half[:, :], ALU.pow).then_inc(s.rs_ready, 1)

        pool.wait_ge(s.acc_zeroed, 3)
        pool.wait_ge(s.unit_read, unit(T_QKV + 15, 1) + 1)
        for c in range(2):
            chunk_step(0, c)
        pool.wait_ge(s.o_ready, 16)
        for p in range(2):
            g.memset(kwv[:, p, CH + DV:CH + DV + 1], 1.0).then_inc(s.core_consts, 1)
        pool.wait_ge(s.core_consts, 2)
        for c in range(2, NCH):
            chunk_step(0, c)
        with pool.Fori(1, HEADS) as h:
            for c in range(NCH):
                chunk_step(h, c)
        for c in range(2):
            chunk_step(HEADS, c)

    @blk.tensor
    def _(pe):
        mmul = nc.tensor.matmul
        pe.wait_ge(s.consts, 5)
        for t in range(KD):
            pe.wait_ge(x_loaded[t], 16)
            for part in range(2):
                k = 2 * t + part
                if k >= 4:
                    pe.wait_ge(s.xt_read, k - 3)
                for b in range(4):
                    last = nc.tensor.transpose(bank[k % 4][:, b * P:(b + 1) * P],
                                               x_tok[:, t, (4 * part + b) * P:(4 * part + b + 1) * P], ident[:, :])
                last.then_inc(s.xt_done, 1)
        pe.wait_ge(s.gains_loaded, 16 * 7)
        nc.tensor.transpose(bank[7][:, 0:56], gain_rows[0:56, :], ident[0:56, 0:56]).then_inc(s.gains_t, 1)

        def stats(index):
            for half in range(2):
                pe.wait_ge(s.acc_done, 2 * KD * (index + 1) - 1 + half)
                mmul(bank[4 + half][:, :], ones[:, :], acc[:, halves[half]], start=True, stop=True) \
                    .then_inc(s.stat_done, 1)

        def pool_block(c):
            g = c // 2
            for half in range(2):
                k = 2 * c + half
                b = bank[4 + k % 4]
                if k >= 4:
                    pe.wait_ge(s.pool_ready, k - 3)
                mmul(b[:, :], zero_row[0:1, 0:P], zero_row[0:1, :], start=True, stop=False)
                if half:
                    mmul(b[:, 0:LONGEST], x_tok[:, 3, c * P:(c + 1) * P], win_main[:, g, P:], start=False, stop=False)
                for t in range(4):
                    tt = 4 * half + t
                    if c == 0:
                        pe.wait_ge(s.xs_ready, tt + 1)
                    width = P + LONGEST if t < 3 else P
                    last = mmul(b[:, t * P:t * P + width], x_tok[:, tt, c * P:(c + 1) * P],
                                (win_main if tt else win_first)[:, g, 0:width], start=False, stop=t == 3)
                last.then_inc(s.pool_done, 1)

        def pool_products(g):
            tile, row = g // 2, 2 * (g % 2)
            pe.wait_ge(s.w_ready, tile + 1)
            for m in range(2):
                for half in range(2):
                    u = 4 * g + 2 * m + half
                    out_bank = pool_unit_bank(u)
                    if g == 0:
                        pe.wait_ge(s.xt_read, 2 * KD)
                    elif g < GROUPS - 1:
                        pe.wait_ge(s.unit_read, u - 3)
                    for k in range(2):
                        pe.wait_ge(s.pool_ready, 2 * (2 * g + k) + half + 1)
                        wh, wl = (w[tile][:, :, :].rearrange("p (a b) m -> p a (b m)", b=2)
                                  [:, row + k, m * P:(m + 1) * P] for w in (whi, wlo))
                        xh, xl = (t[:, 2 * (g % 2) + k, halves[half]] for t in (pool_hi_buf, pool_lo_buf))
                        mmul(out_bank[:, :], wl, xh, start=k == 0, stop=False)
                        mmul(out_bank[:, :], wh, xl, start=False, stop=False)
                        last = mmul(out_bank[:, :], wh, xh, start=False, stop=k == 1)
                    last.then_inc(s.unit_done, 1)

        pe.wait_ge(s.consts, N_CONSTS)
        pe.wait_ge(s.gains_ready, 1)
        for g in range(GROUPS):
            pool_block(2 * g)
            pool_block(2 * g + 1)
            if g:
                pool_products(g - 1)
        pool_products(GROUPS - 1)

        def tile_products(n, par, hi, lo, nb=KD, ready=None, after_half=None, which=(0, 1)):
            pe.wait_ge(s.w_ready, n + 1)
            for half in which:
                b = bank[2 * par + half]
                first = isinstance(n, int) and n == T_FFN0
                pe.wait_ge(s.unit_read, 9 + half if first else 2 * n + (unit(0, half) - 3))
                for k in range(nb):
                    if ready is not None:
                        ready(k, half)
                    xh, xl = hi[:, k, halves[half]], lo[:, k, halves[half]]
                    mmul(b[:, :], wlo[par][:, k, :], xh, start=k == 0, stop=False)
                    mmul(b[:, :], whi[par][:, k, :], xl, start=False, stop=False)
                    last = mmul(b[:, :], whi[par][:, k, :], xh, start=False, stop=k == nb - 1)
                last.then_inc(s.unit_done, 1)
                if after_half is not None:
                    after_half(half)

        def pairs(n0, start, end, *args, **kw):
            with pe.Fori(start, end) as i:
                for part in range(2):
                    tile_products(2 * i + (n0 + part), (n0 + part) % 2, *args, **kw)

        def x_blocks(index):
            return lambda k, half: pe.wait_ge(s.x_ready, 2 * (KD * index + k) + half + 1)

        def ffn(stage, x_index):
            l, n0, j0, nb, first, _ = stage
            if first:
                tile_products(n0, n0 % 2, x_hi_of[l], x_lo_of[l], ready=x_blocks(x_index),
                              after_half=lambda half: stats(x_index) if half == 0 else None)
                tile_products(n0 + 1, (n0 + 1) % 2, x_hi_of[l], x_lo_of[l])
            pairs(n0, int(first), nb, x_hi_of[l], x_lo_of[l])
            j_all = l * NJ + j0
            pairs(n0 + 2 * nb, 0, KD // 2 - (stage is ffn_stages[-1]), a_hi[l], a_lo[l], nb,
                  ready=lambda k, half: pe.wait_ge(s.a_ready, 2 * (j_all + k) + half + 1))

        for st in ffn_stages[:3]:
            ffn(st, 0)

        tile_products(T_GATE, T_GATE % 2, xhi, xlo, ready=x_blocks(1),
                      after_half=lambda half: stats(1) if half == 0 else None)
        pairs(T_QKV, 0, 8, xhi, xlo)
        pe.wait_ge(s.rows_final, 3)
        for kind, rows in enumerate((uu, ww, gi)):
            for c in range(NCH):
                at_col = (kind * NCH + c) * HEADS
                last = nc.tensor.transpose(bank[4][:, at_col:at_col + HEADS], rows[0:HEADS, c * CH:(c + 1) * CH],
                                           ident[0:HEADS, 0:HEADS])
        last.then_inc(s.cols_done, 1)
        pairs(T_O, 0, 4, xhi, xlo)

        def chunk_step(h, c):
            if chunk_ok(h, c, 0):
                i, p = h * NCH + c, c % 2
                pe.wait_ge(s.staged, made(i))
                pe.wait_ge(s.s_ready, freed(i))
                pe.wait_ge(s.v_ready, freed(i))
                mmul(bank[6 + p][:, 0:CH], stage[:, p, 1, :], stage[:, p, 0, :], start=True, stop=True)
                pe.wait_ge(s.v_staged, made(i))
                for b in range(2):
                    last = nc.tensor.transpose(bank[6 + p][:, (b + 1) * CH:(b + 2) * CH], stage[:, p, 2 + b, :],
                                               ident[:, :])
                last.then_inc(s.st_done, 1)
                pe.wait_ge(s.kw_ready, freed(i))
                nc.tensor.transpose(bank[4 + p][:, 0:CH], stage[:, p, 1, :], ident[:, :]).then_inc(s.tr_done, 1)
            if chunk_ok(h, c, 1):
                _, cc, i = lagged(h, c, 1)
                p = cc % 2
                pe.wait_ge(s.s_ready, made(i))
                pe.wait_ge(s.v_ready, made(i))
                pe.wait_ge(s.hn_ready, freed(i))
                num = mmul(bank[p][:, 0:DV + 1], smat[:, p, :], kwv[:, p, CH:], start=True, stop=cc == 0)
                pe.wait_ge(s.kw_ready, made(i))
                pe.wait_ge(s.c_updated, i + SEED)
                pe.wait_ge(s.qs_ready, made(i))
                if cc:
                    num = mmul(bank[p][:, 0:DV + 1], qs[:, p, :], state[:, :], start=False, stop=True)
                num.then_inc(s.num_done, 1)
                mmul(bank[2][:, 0:DV + 1], kwv[:, p, 0:CH], kwv[:, p, CH:], start=True, stop=True) \
                    .then_inc(s.cupd_done, 1)
            if chunk_ok(h, c, 3):
                _, cc, i = lagged(h, c, 3)
                pe.wait_ge(s.hn_ready, made(i))
                pe.wait_ge(s.y_ready, i + SEED)
                for b in range(2):
                    last = nc.tensor.transpose(bank[3][:, b * CH:(b + 1) * CH],
                                               hn[:, cc % 2, b * CH:(b + 1) * CH], ident[:, :])
                last.then_inc(s.ht_done, 1)

        pe.wait_ge(s.unit_read, unit(T_O + 7, 1) + 1)
        pe.wait_ge(s.cols_ready, 1)
        for c in range(NCH):
            chunk_step(0, c)
        with pe.Fori(1, HEADS) as h:
            for c in range(NCH):
                chunk_step(h, c)
        for c in range(3):
            chunk_step(HEADS, c)

        pe.wait_ge(s.y_ready, SEED + HEADS * NCH)
        pe.wait_ge(s.c_updated, SEED + HEADS * NCH)
        pairs(T_OUT, 0, 4, xhi, xlo,
              ready=lambda k, half: pe.wait_ge(s.y_lo, SEED + (k // 2) * NCH + 4 * half + 4))

        for st in ffn_stages[3:]:
            ffn(st, 2)

        def rows_back(t, part):
            if t >= 2:
                pe.wait_ge((s.ft_read_v, s.ft_read_a)[part], t - 1)
            for b in range(4):
                last = nc.tensor.transpose(bank[4 + (2 * t + part) % 4][:, b * P:(b + 1) * P],
                                           x_fin[:, 4 * part + b, t * P:(t + 1) * P], ident[:, :])
            last.then_inc((s.ft_left, s.ft_right)[part], 1)

        def token_stats(half):
            if half == 0:
                pe.wait_ge(s.unit_read, FINAL_UNIT + 1)
            else:
                pe.wait_ge(s.var_tok, 1)
            pe.wait_ge(s.acc_done, 2 * KD * 4 - 2 * (1 - half))
            for t in range(4 * half, 4 * half + 4):
                last = mmul(bank[2][:, t:t + 1], acc[:, t * P:(t + 1) * P], ones[:, 0:1], start=True, stop=True)
            last.then_inc(s.stat_done, 1)

        for idx, (part, half) in enumerate(FINAL_ORDER):
            n = T_END - 2 + part
            tile_products(n, n % 2, a_hi[1], a_lo[1], FFN_BLOCKS[-1][1], which=(half,))
            if idx == 2:
                pe.wait_ge(s.fin_scaled, 2 * KD - 2)
                rows_back(0, 0)
                token_stats(0)
                rows_back(0, 1)
                for part_ in range(2):
                    rows_back(1, part_)
        for t in range(2, 4):
            for part in range(2):
                rows_back(t, part)
        token_stats(1)
        for t in range(4, KD):
            for part in range(2):
                if t == 4 and part == 1:
                    pe.wait_ge(s.fin_scaled, 2 * KD)
                rows_back(t, part)

    @blk.scalar
    def _(act):
        fn = nc.scalar.activation

        def plain_wait():
            act.sem_inc(s.waits_passed, 1)

        def split_hi(n, par):
            act.wait_ge(raw_loaded[par], n * 8 + (16 - 8 * par))
            act.wait_ge(s.unit_done, n * 2 + (unit(0, 1) - 3))
            fn(whi[par][:, :, :], wraw[:, par, :, :], ACT.Copy).then_inc(s.w_hi, 1)

        def square(h, c, half, k, before=2):
            if not isinstance(k, int) or k >= 2:
                act.wait_ge(s.acc_done, k + (1 - before))
            plain_wait()
            fn(blk3(sq[:, half, :]), one(h, c, halves[half]), ACT.Square).then_inc(s.sq_done, 1)

        def root(index):
            for half in range(2):
                act.wait_ge(s.var_ready, 2 * index + half + 1)
                fn(R[:, halves[half]], R[:, halves[half]], ACT.Sqrt).then_inc(s.sd_ready, 1)

        def high_of_x(h, c, half, gain_row, last=False, layer=0):
            plain_wait()
            fn(one(x_fin if last else x_hi_of[layer], c, halves[half]), one(h, c, halves[half]), ACT.Copy,
               scale=gain[:, gain_row, bass.ds(c, 1)]).then_inc(s.fin_scaled if last else s.x_hi, 1)

        for t in range(KD + 3):
            if t < KD:
                act.wait_ge(x_loaded[t], 16)
                if t:
                    act.wait_ge(s.x_ssq, t)
                fn(square_bin[:, :], x_tok[:, t, :], ACT.Square, accum_out=tok_stat[:, 0, t:t + 1]) \
                    .then_inc(s.x_ssq, 1)
            if t >= 3:
                act.wait_ge(s.x_rstd, t - 2)
                act.wait_ge(s.xt_done, 2 * (t - 2))
                fn(x_tok[:, t - 3, :], x_tok[:, t - 3, :], ACT.Copy, scale=tok_stat[:, 1, t - 3:t - 2]) \
                    .then_inc(s.xs_ready, 1)
        for t in range(2):
            act.wait_ge(raw_loaded[t], 16)
            fn(whi[t][:, :, :], wraw[:, t, :, :], ACT.Copy).then_inc(s.w_hi, 1)
        act.wait_ge(s.gains_ready, 1)
        for g in range(GROUPS + 1):
            if g < GROUPS:
                if g >= 2:
                    act.wait_ge(s.unit_done, 4 * (g - 1))
                for c in (2 * g, 2 * g + 1):
                    for half in range(2):
                        k = 2 * c + half
                        act.wait_ge(s.pool_done, k + 1)
                        fn(pool_hi_buf[:, c % 4, halves[half]], bank[4 + k % 4][:, :], ACT.Copy,
                           scale=gain[:, G_POOL, c:c + 1]).then_inc(s.pool_hi, 1)
            if g == GROUPS - 1:
                act.wait_ge(s.unit_done, 8)
                act.wait_ge(raw_loaded[0], 32)
                fn(whi[0][:, :, :], wraw[:, 0, :, :], ACT.Copy).then_inc(s.w_hi, 1)
            if g:
                for c in (2 * g - 2, 2 * g - 1):
                    for half in range(2):
                        act.wait_ge(s.unit_read, 2 * c + half + 1)
                        high_of_x(h0, c, half, G_FFN0)
                        square(h0, c, half, 2 * c + half)

        def ffn_in_pair(stage, j, stat_index=None):
            l, n0 = stage[:2]
            n, par = j * 2 + n0, n0 % 2
            jj = (j + (l * NJ + stage[2])) * 2
            split_hi(n + 1, 1 - par)
            if stat_index is not None:
                root(stat_index)
            for half in range(2):
                act.wait_ge(s.unit_read, n * 2 + (unit(0, half) + 1))
                fn(gate_buf[:, half, :], gate_buf[:, half, :], ACT.Silu).then_inc(s.silu_done, 1)
            split_hi(n + 2, par)
            for half in range(2):
                act.wait_ge(s.unit_read, (n + 1) * 2 + (unit(0, half) + 1))
                plain_wait()
                fn(one(a_hi[l], j, halves[half]), blk3(act_buf[:, half, :]), ACT.Copy).then_inc(s.act_hi, 1)

        def out_pair(n0, i, h, completes, gain_row, sq0, final=False, spill=False):
            for part in range(2):
                n, par = i * 2 + (n0 + part), (n0 + part) % 2
                split_hi(n + 1, 1 - par)
                if completes:
                    for half in range(2):
                        act.wait_ge(s.unit_read, n * 2 + (unit(0, half) + 1))
                        high_of_x(h, i * 2 + part, half, gain_row, final, int(h is h1))
                        square(h, i * 2 + part, half, i * 4 + (sq0 + 2 * part + half))
                    if spill:
                        act.dma_start(h_spill[:, bass.ds(i * 2 + part, 1), :], h[:, bass.ds(i * 2 + part, 1), :]) \
                           .then_inc(s.spilled, 16)

        def ffn(stage, stat_index, gain_row, sq0, final):
            l, n0, j0, nb, first, closes = stage
            if first:
                ffn_in_pair(stage, 0, stat_index)
            with act.Fori(int(first), nb) as j:
                ffn_in_pair(stage, j)
            final = final and closes
            with act.Fori(0, 3 if final else 4) as i:
                out_pair(n0 + 2 * nb, i, h_of[l], closes, gain_row, sq0, final, spill=closes and l == 0)

        for st in ffn_stages[:3]:
            ffn(st, 0, G_MLSTM, 2 * KD, False)

        split_hi(T_QKV, T_QKV % 2)
        root(1)
        split_hi(T_QKV + 1, (T_QKV + 1) % 2)
        act.wait_ge(s.bias_loaded, 32)
        act.wait_ge(s.unit_read, unit(T_GATE, 1) + 1)
        rows = slice(0, HEADS)
        fn(uu[rows, :], lf[rows, :], ACT.Abs, bias=bias_f[rows, :]).then_inc(s.gate_act, 1)
        fn(gi[rows, :], gi[rows, :], ACT.Identity, bias=bias_i[rows, :]).then_inc(s.gate_act, 1)
        act.wait_ge(s.gate_act, 1)
        fn(uu[rows, :], uu[rows, :], ACT.Exp, scale=-1.0).then_inc(s.gate_act, 1)
        act.wait_ge(s.gate_act, 3)
        fn(uu[rows, :], uu[rows, :], ACT.Ln, bias=1.0).then_inc(s.gate_act, 1)
        for n in range(T_QKV + 2, T_QKV + 5):
            split_hi(n, n % 2)
        act.wait_ge(s.gate_chain, GATE_STEPS)
        fn(ri[rows, 1, :], ri[rows, 1, :], ACT.Exp).then_inc(s.rows_final, 1)
        fn(ww[rows, :], ww[rows, :], ACT.Exp).then_inc(s.rows_final, 1)
        fn(gi[rows, :], mm[rows, :], ACT.Exp, scale=-1.0).then_inc(s.rows_final, 1)
        with act.Fori(2, 8) as i:
            for part in range(2):
                n0 = T_QKV + part
                split_hi(i * 2 + (n0 + 1), (n0 + 1) % 2)

        def stage_v(h, c):
            act.wait_ge(s.st_done, freed(h * NCH + c))
            plain_wait()
            fn(stage[:, c % 2, 2:4, :], qkv[:, bass.ds(h * 2 + 2 * HEADS, 2), c * CH:(c + 1) * CH], ACT.Copy) \
                .then_inc(s.v_staged, 1)

        act.wait_ge(s.acc_zeroed, 3)
        act.wait_ge(s.unit_read, unit(T_QKV + 15, 1) + 1)
        for c in range(2):
            stage_v(0, c)
        with act.Fori(0, 4) as i:
            for part in range(2):
                n0 = T_O + part
                split_hi(i * 2 + (n0 + 1), (n0 + 1) % 2)
                for half in range(2):
                    act.wait_ge(s.unit_read, i * 4 + (unit(n0, half) + 1))
                    fn(gate_buf[:, half, :], gate_buf[:, half, :], ACT.Sigmoid).then_inc(s.o_sig, 1)

        def chunk_step(h, c):
            if chunk_ok(h, c, 0):
                i, p = h * NCH + c, c % 2
                if not (isinstance(h, int) and i < 2):
                    stage_v(h, c)
                act.wait_ge(s.z_ready, made(i))
                fn(dmat[:, p, :], dmat[:, p, :], ACT.Exp).then_inc(s.d_ready, 1)
            if chunk_ok(h, c, 1):
                hh, cc, i = lagged(h, c, 1)
                p = cc % 2
                act.wait_ge(s.tr_done, made(i))
                act.wait_ge(s.cupd_done, freed(i))
                plain_wait()
                fn(kwv[:, p, 0:CH], bank[4 + p][:, 0:CH], ACT.Copy, scale=cols[:, 1, cc, bass.ds(hh, 1)]) \
                    .then_inc(s.kw_ready, 1)
            if chunk_ok(h, c, 2):
                _, cc, i = lagged(h, c, 2)
                p = cc % 2
                act.wait_ge(s.num_done, made(i))
                act.wait_ge(s.rs_ready, freed(i))
                fn(tiny[:, p, 0:1], bank[p][:, DV:DV + 1], ACT.Square, scale=EPS ** 0.5).then_inc(s.den_ready, 1)
                act.wait_ge(s.ssq_ready, i + SEED)
                fn(core_bin[:, :], bank[p][:, 0:DV], ACT.Square, scale=DV ** -0.5, accum_out=tiny[:, p, 1:2]) \
                    .then_inc(s.ssq_ready, 1)
            if chunk_ok(h, c, 3):
                _, cc, i = lagged(h, c, 3)
                p = cc % 2
                act.wait_ge(s.rs_ready, made(i))
                act.wait_ge(s.ht_done, freed(i))
                fn(hn[:, p, :], bank[p][:, 0:DV], ACT.Copy, scale=tiny[:, p, 3:4]).then_inc(s.hn_ready, 1)
            if chunk_ok(h, c, 4):
                hh, cc, i = lagged(h, c, 4)
                act.wait_ge(s.y_ready, made(i))
                plain_wait()
                fn(xhi[:, bass.ds(hh * 2, 2), cc * CH:(cc + 1) * CH], yt[:, cc % 2, :, :], ACT.Copy) \
                    .then_inc(s.y_hi, 1)

        act.wait_ge(s.cols_ready, 1)
        act.wait_ge(s.core_consts, 2)
        act.wait_ge(s.unit_done, unit(T_O + 7, 1) + 1)
        for c in range(NCH):
            chunk_step(0, c)
        with act.Fori(1, HEADS) as h:
            for c in range(NCH):
                chunk_step(h, c)
        for c in range(4):
            chunk_step(HEADS, c)

        act.wait_ge(s.acc_zeroed, 4)
        with act.Fori(0, 4) as i:
            out_pair(T_OUT, i, h1, True, G_FFN1, 2 * KD * 2)
        for st in ffn_stages[3:]:
            ffn(st, 2, G_FINAL, 2 * KD * 3, True)

        def final_rows(tiles):
            for t in tiles:
                act.wait_ge(s.ft_right, t + 1)
                fn(out_rows[:, t, HALF:], bank[4 + (2 * t + 1) % 4][:, :], ACT.Copy, scale=rstd_tok[:, t:t + 1]) \
                    .then_inc(s.ft_read_a, 1)

        def final_root(half):
            act.wait_ge(s.var_tok, half + 1)
            fn(rstd_tok[:, 4 * half:4 * half + 4], rstd_tok[:, 4 * half:4 * half + 4], ACT.Sqrt) \
                .then_inc(s.sd_tok, 1)
            act.wait_ge(s.rstd_tok_ready, half + 1)

        split_hi(T_END - 1, (T_END - 1) % 2)
        for idx, (part, half) in enumerate(FINAL_ORDER):
            act.wait_ge(s.unit_read, FINAL_UNIT + idx + 1)
            high_of_x(h1, KD - 2 + part, half, G_FINAL, True)
            square(h1, KD - 2 + part, half, 2 * KD * 4 - 4 + idx, 2 - part)
            if idx == 2:
                final_root(0)
                final_rows((0, 1))
        final_rows((2, 3))
        final_root(1)
        final_rows(range(4, KD))

    @blk.vector
    def _(dve):
        v = nc.vector

        def split_lo(n, par):
            dve.wait_ge(s.w_hi, n + 1)
            v.tensor_tensor(wlo[par][:, :, :], wraw[:, par, :, :], whi[par][:, :, :].bitcast(F32), ALU.subtract) \
             .then_inc(s.w_ready, 1)

        def add_square(half, k, before=2):
            dve.wait_ge(s.sq_done, k + 1)
            dve.wait_ge(s.acc_done, k + (1 - before))
            v.tensor_tensor(acc[:, halves[half]], acc[:, halves[half]], sq[:, half, :], ALU.add) \
             .then_inc(s.acc_done, 1)

        def rstd(index, after_half=None):
            for half in range(2):
                dve.wait_ge(s.stat_done, 2 * index + half + 1)
                v.tensor_scalar(R[:, halves[half]], bank[4 + half][:, :], 1.0 / D, EPS, ALU.mult, ALU.add) \
                 .then_inc(s.var_ready, 1)
            for half in range(2):
                dve.wait_ge(s.sd_ready, 2 * index + half + 1)
                v.reciprocal(R[:, halves[half]], R[:, halves[half]]).then_inc(s.rstd_ready, 1)
                if after_half is not None:
                    dve.wait_ge(s.rstd_ready, 2 * index + half + 1)
                    after_half(half)
            v.memset(acc[:, :], 0.0).then_inc(s.acc_zeroed, 1)
            dve.wait_ge(s.rstd_ready, 2 * index + 2)
            dve.wait_ge(s.acc_zeroed, index + 2 + (index > 1))

        v.memset(acc[:, :], 0.0).then_inc(s.acc_zeroed, 1)
        for t in range(KD):
            dve.wait_ge(s.x_ssq, t + 1)
            v.tensor_scalar(tok_stat[:, 0, t:t + 1], tok_stat[:, 0, t:t + 1], 1.0 / D, EPS, ALU.mult, ALU.add) \
             .then_inc(s.x_var, 1)
            for part in range(2):
                k = 2 * t + part
                dve.wait_ge(s.xt_done, k + 1)
                v.tensor_copy(h0[:, 4 * part:4 * part + 4, t * P:(t + 1) * P],
                              bank[k % 4][:, :].rearrange("p (a b) -> p a b", a=4)).then_inc(s.xt_read, 1)
            if t == 4:
                dve.wait_ge(s.consts, 5 + 4 * GROUPS)
                for gr in range(GROUPS):
                    for m in (win_main, win_first):
                        v.tensor_tensor(m[:, gr, 0:P], m[:, gr, 0:P], ident[:, :], ALU.subtract) \
                         .then_inc(s.consts, 1)
        dve.wait_ge(s.gains_t, 1)
        v.tensor_copy(gain[:, :, :].rearrange("p a b -> p (a b)"), bank[7][:, 0:56]).then_inc(s.gains_ready, 1)
        split_lo(0, 0)
        split_lo(1, 1)
        dve.wait_ge(s.gains_ready, 1)
        dve.wait_ge(s.xt_read, 2 * KD)

        def low_of_x(h, c, half, gain_row, k, layer=0):
            dve.wait_ge(s.x_hi, k + 1)
            v.scalar_tensor_tensor(one(x_lo_of[layer], c, halves[half]), one(h, c, halves[half]),
                                   gain[:, gain_row, bass.ds(c, 1)],
                                   one(x_hi_of[layer], c, halves[half]).bitcast(F32), ALU.mult, ALU.subtract) \
             .then_inc(s.x_ready, 1)

        for g in range(GROUPS + 1):
            if g < GROUPS:
                for c in (2 * g, 2 * g + 1):
                    for half in range(2):
                        k = 2 * c + half
                        dve.wait_ge(s.pool_hi, k + 1)
                        v.scalar_tensor_tensor(pool_lo_buf[:, c % 4, halves[half]], bank[4 + k % 4][:, :],
                                               gain[:, G_POOL, c:c + 1],
                                               pool_hi_buf[:, c % 4, halves[half]].bitcast(F32),
                                               ALU.mult, ALU.subtract).then_inc(s.pool_ready, 1)
            if g == GROUPS - 1:
                split_lo(T_FFN0, 0)
            if g:
                for c in (2 * g - 2, 2 * g - 1):
                    for half in range(2):
                        u = 2 * c + half
                        dve.wait_ge(s.unit_done, u + 1)
                        hv = h0[:, c, halves[half]]
                        v.scalar_tensor_tensor(hv, pool_unit_bank(u)[:, :], gain[:, G_SCALE, c:c + 1], hv,
                                               ALU.mult, ALU.add).then_inc(s.unit_read, 1)
                        dve.wait_ge(s.unit_read, u + 1)
                        low_of_x(h0, c, half, G_FFN0, u)

        def unit_bank(n0, half):
            return bank[2 * (n0 % 2) + half]

        def ffn_in_pair(stage, j, stat_index=None):
            l, n0 = stage[:2]
            n, par = j * 2 + n0, n0 % 2
            jj = (j + (l * NJ + stage[2])) * 2
            split_lo(n + 1, 1 - par)
            if stat_index is not None:
                rstd(stat_index)
            for half in range(2):
                dve.wait_ge(s.unit_done, n * 2 + (unit(0, half) + 1))
                v.tensor_tensor(gate_buf[:, half, :], bank[2 * par + half][:, :], R[:, halves[half]], ALU.mult) \
                 .then_inc(s.unit_read, 1)
            split_lo(n + 2, par)
            for half in range(2):
                dve.wait_ge(s.silu_done, jj + (half + 1))
                v.tensor_tensor(gate_buf[:, half, :], gate_buf[:, half, :], R[:, halves[half]], ALU.mult) \
                 .then_inc(s.silu_scaled, 1)
            for half in range(2):
                dve.wait_ge(s.unit_done, (n + 1) * 2 + (unit(0, half) + 1))
                dve.wait_ge(s.silu_scaled, jj + (half + 1))
                v.tensor_tensor(act_buf[:, half, :], bank[2 * (1 - par) + half][:, :], gate_buf[:, half, :],
                                ALU.mult).then_inc(s.unit_read, 1)
                dve.wait_ge(s.act_hi, jj + (half + 1))
                v.tensor_tensor(one(a_lo[l], j, halves[half]), blk3(act_buf[:, half, :]),
                                one(a_hi[l], j, halves[half]).bitcast(F32), ALU.subtract).then_inc(s.a_ready, 1)

        def out_pair(n0, i, h, completes, gain_row, x0, sq0, final=False):
            for part in range(2):
                n, par = i * 2 + (n0 + part), (n0 + part) % 2
                c = i * 2 + part
                split_lo(n + 1, 1 - par)
                for half in range(2):
                    dve.wait_ge(s.unit_done, n * 2 + (unit(0, half) + 1))
                    v.tensor_tensor(one(h, c, halves[half]), blk3(bank[2 * par + half][:, :]),
                                    one(h, c, halves[half]), ALU.add).then_inc(s.unit_read, 1)
                    if completes:
                        dve.wait_ge(s.unit_read, n * 2 + (unit(0, half) + 1))
                        if not final:
                            low_of_x(h, c, half, gain_row, i * 4 + (x0 + 2 * part + half), int(h is h1))
                        add_square(half, i * 4 + (sq0 + 2 * part + half))

        def ffn(stage, stat_index, gain_row, x0, sq0, final):
            l, n0, j0, nb, first, closes = stage
            if first:
                ffn_in_pair(stage, 0, stat_index)
            with dve.Fori(int(first), nb) as j:
                ffn_in_pair(stage, j)
            final = final and closes
            with dve.Fori(0, 3 if final else 4) as i:
                out_pair(n0 + 2 * nb, i, h_of[l], closes, gain_row, x0, sq0, final)

        for st in ffn_stages[:3]:
            ffn(st, 0, G_MLSTM, 2 * KD, 2 * KD, False)

        split_lo(T_QKV, T_QKV % 2)
        rows = slice(0, HEADS)
        dve.wait_ge(s.spilled, 16 * KD)
        b_gate = [bank[2 * (T_GATE % 2) + half] for half in range(2)]

        def gates_scaled(half):
            hs = halves[half]
            dve.wait_ge(s.unit_done, unit(T_GATE, half) + 1)
            v.tensor_tensor(gi[rows, hs], b_gate[half][0:HEADS, :], R[0:HEADS, hs], ALU.mult)
            v.tensor_tensor(lf[rows, hs], b_gate[half][32:32 + HEADS, :], R[32:32 + HEADS, hs], ALU.mult) \
             .then_inc(s.unit_read, 1)

        rstd(1, gates_scaled)
        gsteps = [0]

        def glink(ins):
            gsteps[0] += 1
            ins.then_inc(s.gate_chain, 1)
            dve.wait_ge(s.gate_chain, gsteps[0])

        def by_chunk(ap):
            return ap.rearrange("p (c t) -> p c t", t=CH)

        def gates_log():
            dve.wait_ge(s.gate_act, 1)
            dve.wait_ge(s.bias_loaded, 32)
            glink(v.tensor_scalar(lf[rows, :], lf[rows, :], bias_f[rows, :], 0.0, ALU.add, ALU.min))
            dve.wait_ge(s.gate_act, 4)
            glink(v.tensor_tensor(lf[rows, :], lf[rows, :], uu[rows, :], ALU.subtract))
            glink(v.memset(ww[rows, :], 1.0))
            glink(v.memset(by_chunk(ww[rows, :])[:, :, 0:1], 0.0))

        def gates_scan():
            glink(v.tensor_tensor_scan(bb[rows, :], ww[rows, :], lf[rows, :], 0.0, ALU.mult, ALU.add))
            glink(v.tensor_tensor_scan(mm[rows, :], lf[rows, :], gi[rows, :], 0.0, ALU.add, ALU.max))

        def gates_rows():
            glink(v.tensor_tensor(ri[rows, 0, :], bb[rows, :], mm[rows, :], ALU.subtract))
            glink(v.tensor_tensor(uu[rows, :], gi[rows, :], bb[rows, :], ALU.subtract))
            glink(v.memset(m_prev[rows, 0:1], 0.0))
            glink(v.tensor_copy(m_prev[rows, 1:NCH], by_chunk(mm[rows, :])[:, 0:NCH - 1, CH - 1]))

        def gates_logs():
            glink(v.tensor_tensor(by_chunk(ri[rows, 1, :]), by_chunk(ri[rows, 0, :]),
                                  m_prev[rows, :].rearrange("p (c a) -> p c a", a=1)
                                  .to_broadcast([HEADS, NCH, CH]), ALU.add))
            glink(v.tensor_tensor(by_chunk(ww[rows, :]), by_chunk(uu[rows, :]),
                                  by_chunk(ri[rows, 0, :])[:, :, CH - 1:CH].to_broadcast([HEADS, NCH, CH]),
                                  ALU.add))

        def qkv_tile(i, part, gate_part=None):
            n0 = T_QKV + part
            split_lo(i * 2 + (n0 + 1), (n0 + 1) % 2)
            if gate_part is not None:
                gate_part()
            for half in range(2):
                dve.wait_ge(s.unit_done, i * 4 + (unit(n0, half) + 1))
                v.tensor_tensor(one(qkv, i * 2 + part, halves[half]), blk3(unit_bank(n0, half)[:, :]),
                                blk3(R[:, halves[half]]), ALU.mult).then_inc(s.unit_read, 1)

        qkv_tile(0, 0, gates_log)
        qkv_tile(0, 1, gates_scan)
        qkv_tile(1, 0, gates_rows)
        qkv_tile(1, 1, gates_logs)
        assert gsteps[0] == GATE_STEPS
        with dve.Fori(2, 8) as i:
            for part in range(2):
                qkv_tile(i, part)
        dve.wait_ge(s.cols_done, 1)
        v.tensor_copy(cols[:, :, :, :].rearrange("p a b c -> p (a b c)"), bank[4][:, 0:3 * NCH * HEADS]) \
         .then_inc(s.cols_read, 1)
        dve.wait_ge(s.cols_read, 1)
        v.scalar_tensor_tensor(cols[:, 2, :, :], cols[:, 2, :, :], EPS, cols[:, 2, :, :], ALU.mult, ALU.mult) \
         .then_inc(s.cols_read, 1)
        dve.wait_ge(s.cols_read, 2)
        v.tensor_scalar(cols[:, 2, :, :], cols[:, 2, :, :], TINY, None, ALU.add).then_inc(s.cols_ready, 1)
        dve.wait_ge(s.rows_out, 16)
        with dve.Fori(0, 4) as i:
            for part in range(2):
                n0 = T_O + part
                split_lo(i * 2 + (n0 + 1), (n0 + 1) % 2)
                for half in range(2):
                    dve.wait_ge(s.unit_done, i * 4 + (unit(n0, half) + 1))
                    v.tensor_tensor(gate_buf[:, half, :], unit_bank(n0, half)[:, :], R[:, halves[half]], ALU.mult) \
                     .then_inc(s.unit_read, 1)
                    dve.wait_ge(s.o_sig, i * 4 + (2 * part + half + 1))
                    v.tensor_scalar(one(sig_o, i * 2 + part, halves[half]), blk3(gate_buf[:, half, :]),
                                    gain[:, G_HEAD, bass.ds(i * 2 + part, 1)], None, ALU.mult) \
                     .then_inc(s.o_ready, 1)

        def chunk_step(h, c):
            if chunk_ok(h, c, 0):
                i, p = h * NCH + c, c % 2
                dve.wait_ge(s.s_ready, freed(i))
                dve.wait_ge(bc_loaded[c % 4], h * 32 + 16 * (c // 4 + 1))
                v.scalar_tensor_tensor(dmat[:, p, :], bc[:, c % 4, 0, :], cols[:, 0, c, bass.ds(h, 1)],
                                       causal[:, :], ALU.add, ALU.add).then_inc(s.z_ready, 1)
            if chunk_ok(h, c, 1):
                _, cc, i = lagged(h, c, 1)
                p = cc % 2
                dve.wait_ge(s.staged, made(i))
                dve.wait_ge(s.num_done, freed(i))
                v.scalar_tensor_tensor(qs[:, p, :], stage[:, p, 0, :], QSCALE, bc[:, cc % 4, 1, :],
                                       ALU.mult, ALU.mult).then_inc(s.qs_ready, 1)
                dve.wait_ge(s.st_done, made(i))
                dve.wait_ge(s.cupd_done, freed(i))
                v.tensor_copy(kwv[:, p, CH:CH + DV], bank[6 + p][:, CH:CH + DV]).then_inc(s.v_ready, 1)
            if chunk_ok(h, c, 2):
                _, cc, i = lagged(h, c, 2)
                dve.wait_ge(s.cupd_done, made(i))
                dve.wait_ge(s.c_updated, i + SEED)
                if cc:
                    v.scalar_tensor_tensor(state[:, :], state[:, :], bc[:, cc % 4, 1, CH - 1:CH],
                                           bank[2][:, 0:DV + 1], ALU.mult, ALU.add).then_inc(s.c_updated, 1)
                else:
                    v.tensor_copy(state[:, :], bank[2][:, 0:DV + 1]).then_inc(s.c_updated, 1)
            if chunk_ok(h, c, 1):
                _, cc, i = lagged(h, c, 1)
                p = cc % 2
                dve.wait_ge(s.d_ready, made(i))
                v.scalar_tensor_tensor(smat[:, p, :], bank[6 + p][:, 0:CH], QSCALE, dmat[:, p, :],
                                       ALU.mult, ALU.mult).then_inc(s.s_ready, 1)
            if chunk_ok(h, c, 4):
                hh, cc, i = lagged(h, c, 4)
                dve.wait_ge(s.ht_done, made(i))
                dve.wait_ge(s.y_lo, freed(i))
                v.tensor_tensor(yt[:, cc % 2, :, :], bank[3][:, 0:DV].rearrange("p (a t) -> p a t", a=2),
                                sig_o[:, bass.ds(hh * 2, 2), cc * CH:(cc + 1) * CH], ALU.mult) \
                 .then_inc(s.y_ready, 1)
            if chunk_ok(h, c, 5):
                hh, cc, i = lagged(h, c, 5)
                tok = slice(cc * CH, (cc + 1) * CH)
                dve.wait_ge(s.y_hi, made(i))
                v.tensor_tensor(xlo[:, bass.ds(hh * 2, 2), tok], yt[:, cc % 2, :, :],
                                xhi[:, bass.ds(hh * 2, 2), tok].bitcast(F32), ALU.subtract).then_inc(s.y_lo, 1)

        dve.wait_ge(s.cols_ready, 1)
        dve.wait_ge(s.o_ready, 16)
        for c in range(NCH):
            chunk_step(0, c)
        with dve.Fori(1, HEADS) as h:
            for c in range(NCH):
                chunk_step(h, c)
        for c in range(5):
            chunk_step(HEADS, c)

        dve.wait_ge(s.y_hi, SEED + HEADS * NCH)
        dve.wait_ge(s.y_lo, SEED + HEADS * NCH)
        v.memset(acc[:, :], 0.0).then_inc(s.acc_zeroed, 1)
        dve.wait_ge(s.acc_zeroed, 4)
        dve.wait_ge(s.h_back, 16)
        with dve.Fori(0, 4) as i:
            out_pair(T_OUT, i, h1, True, G_FFN1, 2 * KD * 2, 2 * KD * 2)
        for st in ffn_stages[3:]:
            ffn(st, 2, G_FINAL, None, 2 * KD * 3, True)

        def final_rows(tiles):
            for t in tiles:
                dve.wait_ge(s.ft_left, t + 1)
                v.tensor_scalar(out_rows[:, t, 0:HALF], bank[4 + (2 * t) % 4][:, :], rstd_tok[:, t:t + 1], None,
                                ALU.mult).then_inc(s.ft_read_v, 1)

        def final_rstd(half):
            r = rstd_tok[:, 4 * half:4 * half + 4]
            dve.wait_ge(s.stat_done, 7 + half)
            v.tensor_scalar(r, bank[2][:, 4 * half:4 * half + 4], 1.0 / D, EPS, ALU.mult, ALU.add) \
             .then_inc(s.var_tok, 1)
            dve.wait_ge(s.sd_tok, half + 1)
            v.reciprocal(r, r).then_inc(s.rstd_tok_ready, 1)
            dve.wait_ge(s.rstd_tok_ready, half + 1)

        split_lo(T_END - 1, (T_END - 1) % 2)
        for idx, (part, half) in enumerate(FINAL_ORDER):
            dve.wait_ge(s.unit_done, FINAL_UNIT + idx + 1)
            hv = h1[:, KD - 2 + part, halves[half]]
            v.tensor_tensor(hv, bank[2 * ((T_END - 2 + part) % 2) + half][:, :], hv, ALU.add) \
             .then_inc(s.unit_read, 1)
            add_square(half, 2 * KD * 4 - 4 + idx, 2 - part)
            if idx == 2:
                final_rstd(0)
                final_rows((0, 1))
        final_rows((2, 3))
        final_rstd(1)
        final_rows(range(4, KD))

    block.__exit__(None, None, None)


_INS = ["x", "pool_norm", "pool_w", "pool_scale", "mlstm_norm", "mlstm_w_in", "mlstm_gate_bias",
        "mlstm_head_norm", "mlstm_w_out", "ffn_norm", "ffn_w_in", "ffn_w_out", "final_norm"]
_OUTS = [((1, NT, D), "float32")]


def kernel(**inputs):
    import numpy as _np
    import concourse.bacc as _bacc
    from concourse import mybir as _mybir
    from concourse.bass_utils import run_bass_kernel_spmd as _run

    nc = _bacc.Bacc("TRN2", target_bir_lowering=False, num_devices=1)
    arrays, args = {}, []
    for name in _INS:
        a = _np.ascontiguousarray(inputs[name])
        arrays[f"in_{name}_dram"] = a
        args.append(nc.dram_tensor(f"in_{name}_dram", a.shape, _mybir.dt.from_np(a.dtype), kind="ExternalInput").ap())
    for i, (shape, dtype) in enumerate(_OUTS):
        dt = _mybir.dt.from_np(_np.dtype(dtype))
        args.append(nc.dram_tensor(f"out_{i}_dram", shape, dt, kind="ExternalOutput").ap())
    build(nc, *args)
    r = _run(nc, [arrays], core_ids=[0])
    got = tuple(r.results[0][f"out_{i}_dram"] for i in range(len(_OUTS)))
    return got[0]
```
